# Optimizing a Trainium2 kernel written in Bass

```python
import math
import jax, jax.numpy as jnp
from jax import lax
import numpy as np

D_MODEL = 1024
BATCH = 1
SEQ = 256
DEPTH = 1

MOBA_HEADS = 8
MOBA_HEAD_DIM = 128
MOBA_WIDTH = MOBA_HEADS * MOBA_HEAD_DIM
MOBA_BLOCK = 256
MOBA_TOPK = 3
MOBA_QUERY_CHUNK = 64
DN_HEADS = 8
DN_KEY_DIM = 128
DN_VALUE_DIM = 128
DN_QK = DN_HEADS * DN_KEY_DIM
DN_V = DN_HEADS * DN_VALUE_DIM
DN_CONV = 4
DN_CHUNK = 64
IN_SIZES = (MOBA_WIDTH, MOBA_WIDTH, MOBA_WIDTH, DN_QK, DN_QK, DN_V, DN_V, DN_HEADS, DN_HEADS, D_MODEL, D_MODEL)
IN_WIDTH = sum(IN_SIZES)
N_EXPERTS = 64
N_GROUPS = 8
TOPK_GROUPS = 4
TOP_K = 8
EXPERT_DIM = 256
SHARED_DIM = 256
ROUTED_SCALE = 2.5
DISPATCH_BLOCK = 128
LN_EPS = 1e-5
RMS_EPS = 1e-6
L2_EPS = 1e-6
DEEPNORM_ALPHA = (2 * DEPTH) ** 0.25
DEEPNORM_BETA = (8 * DEPTH) ** -0.25

kernel_name = "moba_gdn_gated_merge_moe_deepnorm"

def layer_norm(x, g, b):
    xf = x.astype(jnp.float32)
    mu = jnp.mean(xf, axis=-1, keepdims=True)
    xc = xf - mu
    var = jnp.mean(xc * xc, axis=-1, keepdims=True)
    y = xc * lax.rsqrt(var + LN_EPS) * g.astype(jnp.float32) + b.astype(jnp.float32)
    return y.astype(x.dtype)

def l2norm(x):
    return x * lax.rsqrt(jnp.sum(x * x, axis=-1, keepdims=True) + L2_EPS)

def moba_attention(q, k, v):
    B, S, H, Dh = q.shape
    BLK, CQ = MOBA_BLOCK, MOBA_QUERY_CHUNK
    Sp = -(-S // BLK) * BLK
    if Sp != S:
        pad = ((0, 0), (0, Sp - S), (0, 0), (0, 0))
        q, k, v = jnp.pad(q, pad), jnp.pad(k, pad), jnp.pad(v, pad)
    NB = Sp // BLK
    NC = Sp // CQ
    qh = q.transpose(0, 2, 1, 3)
    kb = k.transpose(0, 2, 1, 3).reshape(B, H, NB, BLK, Dh)
    vb = v.transpose(0, 2, 1, 3).reshape(B, H, NB, BLK, Dh)
    kmean = jnp.mean(kb.astype(jnp.float32), axis=3)
    gate = jnp.einsum('bhsd,bhnd->bhsn', qh.astype(jnp.float32), kmean)
    qblk = jnp.arange(Sp) // BLK
    past = jnp.arange(NB)[None, :] < qblk[:, None]
    gate = jnp.where(past, gate, -jnp.inf)
    nsel = min(MOBA_TOPK, NB)
    _, sel = lax.top_k(gate, nsel)
    valid = sel < qblk[None, None, :, None]

    def chunks(t):
        return t.reshape(B, H, NC, CQ, t.shape[-1]).transpose(0, 2, 1, 3, 4).reshape(B * NC, H, CQ, t.shape[-1])

    q_c, sel_c, valid_c = chunks(qh), chunks(sel), chunks(valid)
    b_id = jnp.repeat(jnp.arange(B, dtype=jnp.int32), NC)
    c_id = jnp.tile(jnp.arange(NC, dtype=jnp.int32), B)
    scale = Dh ** -0.5
    key_off = jnp.arange(BLK)
    q_off = jnp.arange(CQ)
    h_ix = jnp.arange(H)[:, None, None]

    def attend(args):
        qc, sc, vc, b, c = args
        kbb, vbb = kb[b], vb[b]
        ksel = kbb[h_ix, sc]
        vsel = vbb[h_ix, sc]
        j = (c * CQ) // BLK
        kown, vown = kbb[:, j], vbb[:, j]
        s_sel = jnp.einsum('hqd,hqnkd->hqnk', qc, ksel, preferred_element_type=jnp.float32) * scale
        s_sel = jnp.where(vc[..., None], s_sel, -jnp.inf).reshape(H, CQ, nsel * BLK)
        s_own = jnp.einsum('hqd,hkd->hqk', qc, kown, preferred_element_type=jnp.float32) * scale
        causal = (j * BLK + key_off)[None, :] <= (c * CQ + q_off)[:, None]
        s_own = jnp.where(causal[None], s_own, -jnp.inf)
        p = jax.nn.softmax(jnp.concatenate([s_sel, s_own], axis=-1), axis=-1)
        p_sel = p[..., :nsel * BLK].reshape(H, CQ, nsel, BLK).astype(vsel.dtype)
        p_own = p[..., nsel * BLK:].astype(vown.dtype)
        return (jnp.einsum('hqnk,hqnkd->hqd', p_sel, vsel)
                + jnp.einsum('hqk,hkd->hqd', p_own, vown))

    out = lax.map(attend, (q_c, sel_c, valid_c, b_id, c_id))
    out = out.reshape(B, NC, H, CQ, Dh).transpose(0, 1, 3, 2, 4).reshape(B, Sp, H, Dh)
    return out[:, :S]

def causal_depthwise_conv(x, w):
    width, channels = w.shape
    return lax.conv_general_dilated(
        x, w[:, None, :].astype(x.dtype), window_strides=(1,), padding=[(width - 1, 0)],
        dimension_numbers=("NWC", "WIO", "NWC"), feature_group_count=channels)

def chunk_gated_delta_rule(q, k, v, g, beta):
    B, S, H, Dk = q.shape
    Dv = v.shape[-1]
    C = DN_CHUNK
    N = S // C

    def chunks(t):
        return t.reshape(B, N, C, H, t.shape[-1]).transpose(0, 3, 1, 2, 4)

    q, k, v = chunks(q), chunks(k), chunks(v)
    gc = jnp.cumsum(g.reshape(B, N, C, H).transpose(0, 3, 1, 2), axis=-1)
    bt = beta.reshape(B, N, C, H).transpose(0, 3, 1, 2)[..., None]
    kb, vb = k * bt, v * bt
    incl = jnp.tril(jnp.ones((C, C), dtype=bool))
    strict = jnp.tril(jnp.ones((C, C), dtype=bool), -1)
    diff = gc[..., :, None] - gc[..., None, :]
    decay = jnp.where(incl, jnp.exp(jnp.where(incl, diff, 0.0)), 0.0)
    L = jnp.where(strict, jnp.einsum('bhnid,bhnjd->bhnij', kb, k) * decay, 0.0)
    eye = jnp.eye(C, dtype=jnp.float32)
    T = lax.linalg.triangular_solve(L + eye, jnp.broadcast_to(eye, L.shape), left_side=True,
                                    lower=True, unit_diagonal=True)
    u = T @ vb
    w = T @ (kb * jnp.exp(gc)[..., None])
    A = jnp.einsum('bhnid,bhnjd->bhnij', q, k) * decay
    qd = q * jnp.exp(gc)[..., None]
    kd = k * jnp.exp(gc[..., -1:] - gc)[..., None]
    glast = jnp.exp(gc[..., -1])
    xs = (jnp.moveaxis(qd, 2, 0), jnp.moveaxis(kd, 2, 0), jnp.moveaxis(u, 2, 0),
          jnp.moveaxis(w, 2, 0), jnp.moveaxis(A, 2, 0), jnp.moveaxis(glast, 2, 0))

    def step(state, inp):
        qd_i, kd_i, u_i, w_i, a_i, gl_i = inp
        v_new = u_i - jnp.einsum('bhcd,bhde->bhce', w_i, state)
        o = jnp.einsum('bhcd,bhde->bhce', qd_i, state) + jnp.einsum('bhcj,bhje->bhce', a_i, v_new)
        state = state * gl_i[..., None, None] + jnp.einsum('bhcd,bhce->bhde', kd_i, v_new)
        return state, o

    state0 = jnp.zeros((B, H, Dk, Dv), jnp.float32)
    _, o = lax.scan(step, state0, xs)
    return o.transpose(1, 0, 3, 2, 4).reshape(B, S, H, Dv)

def gated_delta_net(q, k, v, z, a, b, conv_w, a_log, dt_bias, norm_w):
    Bsz, S, _ = q.shape
    qkv = jax.nn.silu(causal_depthwise_conv(jnp.concatenate([q, k, v], axis=-1), conv_w))
    qc, kc, vc = jnp.split(qkv, [DN_QK, 2 * DN_QK], axis=-1)
    qf = l2norm(qc.reshape(Bsz, S, DN_HEADS, DN_KEY_DIM).astype(jnp.float32)) * (DN_KEY_DIM ** -0.5)
    kf = l2norm(kc.reshape(Bsz, S, DN_HEADS, DN_KEY_DIM).astype(jnp.float32))
    vf = vc.reshape(Bsz, S, DN_HEADS, DN_VALUE_DIM).astype(jnp.float32)
    beta = jax.nn.sigmoid(b.astype(jnp.float32))
    g = -jnp.exp(a_log.astype(jnp.float32)) * jax.nn.softplus(a.astype(jnp.float32) + dt_bias.astype(jnp.float32))
    o = chunk_gated_delta_rule(qf, kf, vf, g, beta)
    zf = z.reshape(Bsz, S, DN_HEADS, DN_VALUE_DIM).astype(jnp.float32)
    o = o * lax.rsqrt(jnp.mean(o * o, axis=-1, keepdims=True) + RMS_EPS) * norm_w.astype(jnp.float32) * jax.nn.silu(zf)
    return o.reshape(Bsz, S, DN_V).astype(q.dtype)

def token_mixer(x, w_in, conv_w, a_log, dt_bias, norm_w, w_branch_a, w_branch_b, w_out):
    Bsz, S, _ = x.shape
    proj = x @ w_in
    (q_a, k_a, v_a, q_b, k_b, v_b, z_b, a_b, b_b, gate_a, gate_b) = jnp.split(
        proj, np.cumsum(IN_SIZES)[:-1].tolist(), axis=-1)
    heads_a = lambda t: t.reshape(Bsz, S, MOBA_HEADS, MOBA_HEAD_DIM)
    y_a = moba_attention(heads_a(q_a), heads_a(k_a), heads_a(v_a)).reshape(Bsz, S, MOBA_WIDTH)
    y_b = gated_delta_net(q_b, k_b, v_b, z_b, a_b, b_b, conv_w, a_log, dt_bias, norm_w)
    merged = jax.nn.sigmoid(gate_a) * (y_a @ w_branch_a) + jax.nn.sigmoid(gate_b) * (y_b @ w_branch_b)
    return merged @ w_out

def swiglu(x, w_gate, w_up, w_down):
    return (jax.nn.silu(x @ w_gate) * (x @ w_up)) @ w_down

def moe_ffn(x, w_router, router_bias, w_gate_e, w_up_e, w_down_e, w_gate_s, w_up_s, w_down_s):
    Bsz, S, D = x.shape
    xf = x.reshape(-1, D)
    N = xf.shape[0]
    scores = jax.nn.sigmoid(jnp.dot(xf, w_router, preferred_element_type=jnp.float32))
    choice = scores + router_bias.astype(jnp.float32)
    grouped = choice.reshape(N, N_GROUPS, N_EXPERTS // N_GROUPS)
    group_score = jnp.sum(lax.top_k(grouped, 2)[0], axis=-1)
    _, gidx = lax.top_k(group_score, TOPK_GROUPS)
    gmask = jnp.any(gidx[..., None] == jnp.arange(N_GROUPS), axis=1)
    emask = jnp.repeat(gmask, N_EXPERTS // N_GROUPS, axis=1)
    _, eidx = lax.top_k(jnp.where(emask, choice, -jnp.inf), TOP_K)
    wts = jnp.take_along_axis(scores, eidx, axis=1)
    wts = wts / jnp.sum(wts, axis=-1, keepdims=True) * ROUTED_SCALE

    NK = N * TOP_K
    BLK = DISPATCH_BLOCK
    nb = -(-(NK + N_EXPERTS * (BLK - 1)) // BLK)
    P = nb * BLK
    flat_e = eidx.reshape(-1)
    flat_tok = jnp.arange(NK, dtype=jnp.int32) // TOP_K
    flat_w = wts.reshape(-1)
    order = jnp.argsort(flat_e)
    e_sorted = flat_e[order]
    counts = jnp.bincount(flat_e, length=N_EXPERTS)
    padded = (counts + BLK - 1) // BLK * BLK
    start = jnp.cumsum(counts) - counts
    pend = jnp.cumsum(padded)
    pstart = pend - padded
    dest = pstart[e_sorted] + (jnp.arange(NK) - start[e_sorted])
    tok_pad = jnp.full((P,), N, jnp.int32).at[dest].set(flat_tok[order])
    w_pad = jnp.zeros((P,), jnp.float32).at[dest].set(flat_w[order])
    blk_e = jnp.clip(jnp.searchsorted(pend, jnp.arange(nb) * BLK, side='right'), 0, N_EXPERTS - 1)
    x_ext = jnp.concatenate([xf, jnp.zeros((1, D), xf.dtype)], axis=0)

    def expert_block(acc, inp):
        tok, wt, e = inp
        xb = x_ext[tok]
        yb = swiglu(xb, w_gate_e[e], w_up_e[e], w_down_e[e]) * wt[:, None].astype(xb.dtype)
        return acc.at[tok].add(yb), None

    acc, _ = lax.scan(expert_block, jnp.zeros((N + 1, D), x.dtype),
                      (tok_pad.reshape(nb, BLK), w_pad.reshape(nb, BLK), blk_e))
    out = acc[:N] + swiglu(xf, w_gate_s, w_up_s, w_down_s)
    return out.reshape(Bsz, S, D)

def setup_inputs(seed: int = 0) -> dict:
    key = jax.random.key(seed)
    ks = jax.random.split(key, 24)

    def nrm(k, shape, scale):
        return jax.random.normal(k, shape, jnp.float32) * scale

    dt = jnp.exp(jax.random.uniform(ks[4], (DEPTH, DN_HEADS), jnp.float32, math.log(1e-3), math.log(1e-1)))
    return {
        "x": nrm(ks[0], (BATCH, SEQ, D_MODEL), 1.0),
        "w_in": nrm(ks[1], (DEPTH, D_MODEL, IN_WIDTH), D_MODEL ** -0.5),
        "dn_conv_w": nrm(ks[2], (DEPTH, DN_CONV, 2 * DN_QK + DN_V), DN_CONV ** -0.5),
        "dn_a_log": jnp.log(jax.random.uniform(ks[3], (DEPTH, DN_HEADS), jnp.float32, 1.0, 16.0)),
        "dn_dt_bias": jnp.log(jnp.expm1(dt)),
        "dn_norm_w": 1.0 + nrm(ks[5], (DEPTH, DN_VALUE_DIM), 0.02),
        "w_branch_a": nrm(ks[6], (DEPTH, MOBA_WIDTH, D_MODEL), MOBA_WIDTH ** -0.5),
        "w_branch_b": nrm(ks[7], (DEPTH, DN_V, D_MODEL), DN_V ** -0.5),
        "w_out": nrm(ks[8], (DEPTH, D_MODEL, D_MODEL), D_MODEL ** -0.5 * DEEPNORM_BETA),
        "ln1_g": 1.0 + nrm(ks[9], (DEPTH, D_MODEL), 0.02),
        "ln1_b": nrm(ks[10], (DEPTH, D_MODEL), 0.02),
        "w_router": nrm(ks[11], (DEPTH, D_MODEL, N_EXPERTS), D_MODEL ** -0.5),
        "router_bias": nrm(ks[12], (DEPTH, N_EXPERTS), 0.01),
        "w_gate_e": nrm(ks[13], (DEPTH, N_EXPERTS, D_MODEL, EXPERT_DIM), D_MODEL ** -0.5),
        "w_up_e": nrm(ks[14], (DEPTH, N_EXPERTS, D_MODEL, EXPERT_DIM), D_MODEL ** -0.5),
        "w_down_e": nrm(ks[15], (DEPTH, N_EXPERTS, EXPERT_DIM, D_MODEL), EXPERT_DIM ** -0.5 * DEEPNORM_BETA),
        "w_gate_s": nrm(ks[16], (DEPTH, D_MODEL, SHARED_DIM), D_MODEL ** -0.5),
        "w_up_s": nrm(ks[17], (DEPTH, D_MODEL, SHARED_DIM), D_MODEL ** -0.5),
        "w_down_s": nrm(ks[18], (DEPTH, SHARED_DIM, D_MODEL), SHARED_DIM ** -0.5 * DEEPNORM_BETA),
        "ln2_g": 1.0 + nrm(ks[19], (DEPTH, D_MODEL), 0.02),
        "ln2_b": nrm(ks[20], (DEPTH, D_MODEL), 0.02),
    }

def reference(x, w_in, dn_conv_w, dn_a_log, dn_dt_bias, dn_norm_w, w_branch_a, w_branch_b, w_out,
              ln1_g, ln1_b, w_router, router_bias, w_gate_e, w_up_e, w_down_e,
              w_gate_s, w_up_s, w_down_s, ln2_g, ln2_b):
    for l in range(DEPTH):
        mix = token_mixer(x, w_in[l], dn_conv_w[l], dn_a_log[l], dn_dt_bias[l], dn_norm_w[l],
                          w_branch_a[l], w_branch_b[l], w_out[l])
        x = layer_norm(DEEPNORM_ALPHA * x + mix, ln1_g[l], ln1_b[l])
        ffn = moe_ffn(x, w_router[l], router_bias[l], w_gate_e[l], w_up_e[l], w_down_e[l],
                      w_gate_s[l], w_up_s[l], w_down_s[l])
        x = layer_norm(DEEPNORM_ALPHA * x + ffn, ln2_g[l], ln2_b[l])
    return x


_drawn_inputs = setup_inputs


def setup_inputs(seed=0):
    import zlib

    import numpy as np

    out = dict(_drawn_inputs(seed))
    spreads = {}
    factors = {'dn_norm_w': 2.895, 'ln2_g': 2.837, 'ln2_b': 2.949}
    for name, (base, spread) in spreads.items():
        noise = np.random.default_rng([zlib.crc32(name.encode()), seed]).standard_normal(out[name].shape)
        drawn = base * np.exp(spread * noise) if base else spread * noise
        out[name] = __import__('jax').numpy.asarray(drawn.astype(out[name].dtype))
    for name, factor in factors.items():
        out[name] = (out[name] * factor).astype(out[name].dtype)
    return out
```

```python
from contextlib import ExitStack

import numpy as np

import concourse.bass as bass
from concourse import mybir

F32 = mybir.dt.float32
F32R = mybir.dt.float32r
I32 = mybir.dt.int32
BF16 = mybir.dt.bfloat16
ALU = mybir.AluOpType
ACT = mybir.ActivationFunctionType
AX = mybir.AxisListType

P = 128
D = 1024
T = 256
TT = T // P
KC = D // P
H = 8
DH = 128
NE = 64
FE = 256
GROUPS = 8
TOP_G = 4
SLOTS = 64
LEVELS = 7
ALPHA = 2 ** 0.25
LN_EPS = 1e-5
RMS_EPS = 1e-6
L2_EPS = 1e-6
ROUTED_SCALE = 2.5
QK_SCALE = DH ** -0.5
NEG = -1e30

COL = {}
_at = 0
for _name, _n in (("qa", 1024), ("ka", 1024), ("va", 1024), ("qb", 1024), ("kb", 1024), ("vb", 1024), ("z", 1024),
                  ("ab", 16), ("ga", 1024), ("gb", 1024)):
    COL[_name] = _at
    _at += _n

CONST = {}
_at = 0
for _name, _n in (("ident", P), ("tri", P), ("before", P), ("strict", P), ("levels", LEVELS * P),
                  ("causal", 3 * P), ("slot", SLOTS), ("tie", GROUPS * GROUPS)):
    CONST[_name] = (_at, _at + _n)
    _at += _n
NCONST = _at


def constants():
    c = np.zeros((P, NCONST), np.float32)
    r = np.arange(P)
    def put(name, a):
        c[:, CONST[name][0]:CONST[name][1]] = a
    put("ident", np.eye(P))
    put("tri", r[:, None] <= r[None, :])
    put("before", r[:, None] < r[None, :])
    put("strict", r[:, None] > r[None, :])
    levels = []
    for s in range(LEVELS):
        b = 1 << s
        same = (r[:, None] // (2 * b)) == (r[None, :] // (2 * b))
        levels.append(same & ((r[:, None] // b) % 2 == 1) & ((r[None, :] // b) % 2 == 0))
    put("levels", np.concatenate(levels, 1))
    diag = np.where(r[None, :] <= r[:, None], 0.0, NEG)
    put("causal", np.concatenate([diag, np.zeros((P, P)), diag], 1))
    put("slot", np.arange(SLOTS)[None, :])
    g = np.arange(GROUPS)
    put("tie", (g[None, :] < g[:, None]).astype(np.float32).reshape(1, -1))
    return c


class Steps:

    def __init__(self, engine, semaphore):
        self.engine, self.semaphore = engine, semaphore
        self.count, self.trip = 0, None

    def did(self, instruction):
        instruction.then_inc(self.semaphore, 1)
        self.count += 1

    def settle(self):
        value = self.count
        if self.trip is not None:
            value = self.trip[0] * self.trip[1] + self.count
        self.engine.wait_ge(self.semaphore, value)

    def then(self, instruction):
        self.did(instruction)
        self.settle()

    def enter(self, i, per):
        self.trip, self.start = (i, per), self.count

    def leave(self, trips):
        per = self.trip[1]
        assert self.count - self.start == per, (self.count - self.start, per)
        self.count, self.trip = self.start + trips * per, None


def program(nc, x, w_in, dn_conv_w, dn_a_log, dn_dt_bias, dn_norm_w, w_branch_a, w_branch_b, w_out, ln1_g, ln1_b,
            w_router, router_bias, w_gate_e, w_up_e, w_down_e, w_gate_s, w_up_s, w_down_s, ln2_g, ln2_b, table, out):
    with ExitStack() as ctx:
        build(nc, ctx, x, w_in, dn_conv_w, dn_a_log, dn_dt_bias, dn_norm_w, w_branch_a, w_branch_b, w_out, ln1_g,
              ln1_b, w_router, router_bias, w_gate_e, w_up_e, w_down_e, w_gate_s, w_up_s, w_down_s, ln2_g, ln2_b,
              table, out)


def build(nc, ctx, x, w_in, dn_conv_w, dn_a_log, dn_dt_bias, dn_norm_w, w_branch_a, w_branch_b, w_out, ln1_g, ln1_b,
          w_router, router_bias, w_gate_e, w_up_e, w_down_e, w_gate_s, w_up_s, w_down_s, ln2_g, ln2_b, table, out):
    def sem(name):
        return ctx.enter_context(nc.semaphore(name))

    place = {}

    def at(name, shape, offset, dtype=F32):
        t = nc.alloc_sbuf_tensor_at(name, shape, dtype, offset=offset)
        place[name] = offset + -(-int(np.prod(shape[1:])) * (2 if dtype == BF16 else 4) // 32) * 32
        return t

    SLOT = 2048
    RING = 16512
    MIXW = RING + 12 * SLOT * 4
    REST = MIXW + 32768
    ring = at("ring", [P, 12, SLOT], RING)
    mixw = at("mixw", [P, 2, 4, KC, P], MIXW)
    x_nat = at("x_nat", [P, TT, D], REST)
    xT = at("xT", [P, KC, T], place["x_nat"])
    const = at("const", [P, NCONST], place["xT"])
    sga = at("sga", [P, KC, T], place["const"])
    yaT = at("yaT", [P, H, T], place["sga"])
    szT = at("szT", [P, H, T], place["yaT"])
    kT1 = at("kT1", [P, H, P], place["szT"])
    qd1 = at("qd1", [P, H, P], place["kT1"])
    kd0 = at("kd0", [P, H, P], place["qd1"])
    vb = at("vb", [P, TT, H, DH], place["kd0"])
    TEMP = place["vb"]
    acc = at("acc", [P, 3, T], TEMP)
    v_act = at("v_act", [P, T], place["acc"])
    conv_rows = at("conv_rows", [96, P], RING)
    w_ab = at("w_ab", [P, KC, 16], place["conv_rows"])
    kn = at("kn", [P, 2, 2 * T], TEMP)
    qkT = at("qkT", [P, 2, T], TEMP)
    v_nat = at("v_nat", [P, TT, DH], place["qkT"])
    score = at("score", [P, 3, P], place["v_nat"])
    prob = at("prob", [P, 3, P], place["score"])
    probT = at("probT", [P, 3, P], place["prob"])
    gtmp = at("gtmp", [P, 2, T], place["probT"])
    merged = at("merged", [P, 2, T], place["v_nat"])
    SMALL = max(place["v_act"], place["gtmp"])
    conv_w = at("conv_w", [P, 96], SMALL)
    abT = at("abT", [16, T], place["w_ab"])
    ab = at("ab", [P, TT, 16], place["conv_w"])
    dtb = at("dtb", [P, H], place["ab"])
    alog = at("alog", [P, H], place["dtb"])
    normw = at("normw", [P, 1], place["alog"])
    g_u = at("g_u", [P, TT, H], place["normw"])
    g_abs = at("g_abs", [P, TT, H], place["g_u"])
    g_e = at("g_e", [P, TT, 16], place["g_abs"])
    decay_g = at("decay_g", [P, TT, H], place["g_e"])
    beta = at("beta", [P, TT, H], place["decay_g"])
    gcl = at("gcl", [P, 2, TT * H], place["beta"])
    ngc = at("ngc", [P, TT * H], place["gcl"])
    e_last = at("e_last", [P, TT * H], place["ngc"])
    nbeg = at("nbeg", [P, TT * H], place["e_last"])
    smx = at("smx", [P, 8], place["nbeg"])
    eps_l2 = at("eps_l2", [P, 1], place["smx"])
    eps_rms = at("eps_rms", [P, 1], place["eps_l2"])
    one = at("one", [P, 1], place["eps_rms"])
    eps_ln = at("eps_ln", [P, 1], place["one"])
    ones = at("ones", [P, P], place["eps_ln"])
    zeros = at("zeros", [P, 512], place["kd0"], BF16)
    stats = at("stats", [P, TT, 2, 6], place["ones"])
    moment = at("moment", [P, TT, 2], place["stats"])
    END = place["moment"]
    assert END <= nc.sbuf_usable_end, (END, nc.sbuf_usable_end)
    L = at("L", [P, TT, H, P], RING + 6 * SLOT * 4)
    AT = at("AT", [P, TT, H, P], place["L"])
    LM = at("LM", [P, TT, H, P], place["AT"])
    W = at("W", [P, TT, H, P], place["LM"])
    U = at("U", [P, TT, H, P], place["W"])
    TI = at("TI", [P, TT, H, P], place["U"])
    kq = at("kq", [P, H, 2 * T], place["AT"])
    R = at("R", [P, H, DH], place["AT"])
    osq = at("osq", [P, H, T], place["AT"])
    oT = at("oT", [P, H, T], place["LM"])
    V = at("V", [P, TT, H, DH], place["U"])
    S1 = at("S1", [P, H, DH], place["AT"] + 4096)
    sq = at("sq", [P, 2, 2 * T], place["W"])
    rr = at("rr", [P, 2, 2 * T], place["W"] + 4096)
    g_wide = at("g_wide", [P, TT * H, P], place["U"])
    edist = at("edist", [P, TT * H, P], place["W"])

    def c(name, n=None):
        a = const[:, CONST[name][0]:CONST[name][1]]
        return a if n is None else a.rearrange("p (n c) -> p n c", n=n)

    ident = c("ident")

    bank = [ctx.enter_context(nc.psum_tensor(f"bank{i}", [P, 512], F32)) for i in range(8)]

    x_in, early_in, vec_in, ln1_in = sem("x_in"), sem("early_in"), sem("vec_in"), sem("ln1_in")
    mix_in = [[sem(f"mix_in{b}{k}") for k in range(4)] for b in range(2)]
    const_set = sem("const_set")
    x_turned, xT_vec, xT_act = sem("x_turned"), sem("xT_vec"), sem("xT_act")
    ab_done, ab_set = sem("ab_done"), sem("ab_set")
    gate_vec, gate_act = sem("gate_vec"), sem("gate_act")
    cum_done, wide_done, dist_done = sem("cum_done"), sem("wide_done"), sem("dist_done")
    proj_done = sem("proj_done")
    conv_step, act_done = sem("conv_step"), sem("act_done")
    v_turned, vb_done = sem("v_turned"), sem("vb_done")
    sq_done, sumsq_done, norm_act, norm_set = sem("sq_done"), sem("sumsq_done"), sem("norm_act"), sem("norm_set")
    pair_done, pair_set, kd_set = sem("pair_done"), sem("pair_set"), sem("kd_set")
    masked, lm_turned = sem("masked"), sem("lm_turned")
    inv_mm, inv_act, inv_vec = sem("inv_mm"), sem("inv_act"), sem("inv_vec")
    scan_mm, scan_act, scan_vec = sem("scan_mm"), sem("scan_act"), sem("scan_vec")
    rms_act, rms_vec, rms_mm = sem("rms_act"), sem("rms_vec"), sem("rms_mm")
    att_act, att_mm, att_vec = sem("att_act"), sem("att_mm"), sem("att_vec")
    mer_act, mer_vec = sem("mer_act"), sem("mer_vec")
    ln_act, ln_vec = sem("ln_act"), sem("ln_vec")
    out_sent = sem("out_sent")
    load_turn = sem("load_turn")
    rout_in, shared_in, ln2_in = sem("rout_in"), [sem("gate_s_in"), sem("up_s_in"), sem("down_s_in")], sem("ln2_in")
    exp_in = [sem(f"exp_in{n}") for n in range(12)]
    x1_turned, x1T_vec, x1T_act = sem("x1_turned"), sem("x1T_vec"), sem("x1T_act")
    x1hi_set, x1lo_set = sem("x1hi_set"), sem("x1lo_set")
    log_done, logT_set, log_turned, sco_set = sem("log_done"), sem("logT_set"), sem("log_turned"), sem("sco_set")
    rout_step, pos_done = sem("rout_step"), sem("pos_done")
    sh_done, gsh_set, hsT_set, shd_done = sem("sh_done"), sem("gsh_set"), sem("hsT_set"), sem("shd_done")
    clear_set, pick_set, gath_done, xg_set = sem("clear_set"), sem("pick_set"), sem("gath_done"), sem("xg_set")
    gu_done, act_set, hid_set = sem("gu_done"), sem("act_set"), sem("hid_set")
    hid_turned, hidT_set, down_done = sem("hid_turned"), sem("hidT_set"), sem("down_done")
    yhi_set, ylo_set, wp_turned, drop_set = sem("yhi_set"), sem("ylo_set"), sem("wp_turned"), sem("drop_set")
    scat_done, acc_done = sem("scat_done"), sem("acc_done")
    ln2_act, ln2_vec = sem("ln2_act"), sem("ln2_vec")

    w_in_v = w_in[0].rearrange("(k p) n -> p k n", p=P)
    wa_v = w_branch_a[0].rearrange("(k p) n -> p k n", p=P)
    wb_v = w_branch_b[0].rearrange("(k p) n -> p k n", p=P)
    wo_v = w_out[0].rearrange("(k p) n -> p k n", p=P)
    PAIRS, BATCH = NE // 2, 4
    x1r = at("x1r", [P, TT, 2, KC, P], place["const"], F32R)
    yr = at("yr", [P, 2, D], place["x1r"], F32R)
    xg0 = at("xg0", [P, 2, KC, P], place["szT"])
    w_rout = at("w_rout", [P, KC, NE], place["qd1"])
    r_bias = at("r_bias", [P, NE], place["w_rout"])
    pos = at("pos", [P, TT, NE + 2 * BATCH], place["r_bias"])
    wgt = at("wgt", [P, TT, NE + 2 * BATCH], place["pos"])
    xg1 = at("xg1", [P, 2, KC, P], place["kd0"])
    xg = [xg0, xg1]
    pick = at("pick", [P, TT, BATCH * SLOTS], TEMP, F32R)
    wpick = at("wpick", [P, 2, TT, BATCH * SLOTS], place["pick"])
    drop = at("drop", [P, 2, T], place["wpick"], F32R)
    x1T = at("x1T", [P, KC, T], place["x_nat"])
    hid = at("hid", [P, 2, P], place["x_nat"])
    hidT = at("hidT", [P, 2, P], place["hid"])
    gact = at("gact", [P, FE], place["hidT"])
    wslot = at("wslot", [P, 2], place["gact"])
    gsh = at("gsh", [P, 2 * T], place["x1r"])
    hsT = at("hsT", [P, 2, T], place["gsh"])
    w_gu_s = at("w_gu_s", [P, 2, KC, FE], MIXW)
    w_d_s = at("w_d_s", [P, 2, D], place["w_gu_s"])
    ln2v = at("ln2v", [P, 2, D], place["w_d_s"])
    logT = at("logT", [NE, T], place["kd0"])
    sco = at("sco", [P, TT, NE], place["logT"])
    cho = at("cho", [P, TT, NE], place["sco"])
    rep_ = at("rep_", [P, TT, NE], place["cho"])
    selm = at("selm", [P, TT, NE], place["rep_"])
    best = at("best", [P, TT, GROUPS, 8], place["selm"])
    gsc = at("gsc", [P, TT, GROUPS], place["best"])
    gmk = at("gmk", [P, TT, GROUPS], place["gsc"])
    goff = at("goff", [P, TT, GROUPS], place["gmk"])
    cmp1 = at("cmp1", [P, TT, GROUPS, GROUPS], place["goff"])
    cmp2 = at("cmp2", [P, TT, GROUPS, GROUPS], place["cmp1"])
    top = at("top", [P, TT, 8], place["cmp2"])
    wsum = at("wsum", [P, TT], place["top"])
    most = at("most", [P, 1], place["wsum"])
    most_i = at("most_i", [P, 1], SMALL, I32)
    ln1v = at("ln1v", [P, 2, D], place["szT"])

    def tiles_of(phase, h):
        def w(name):
            return w_in_v[:, :, bass.ds(COL[name] + h * P, P)]
        if phase == 0:
            return [w("kb"), w("qb"), w("vb"), w("z")]
        if phase == 1:
            return [w("qa"), w("ka"), w("va"), w("ga")]
        return [w("gb"), wb_v[:, :, bass.ds(h * P, P)], wa_v[:, :, bass.ds(h * P, P)],
                wo_v[:, bass.ds(h, 1), :].rearrange("p a (k c) -> p (a k) c", k=KC)]

    GATE_G, GATE_WIDE, GATE_CUM, GATE_ALL = 5, 6, 11, 14
    DIST_BANKS, SCAN_MM, LN_VEC = 18, 12, 16
    ROUT_SEL, ROUT_MOST = 32, 37
    PASSES = T // SLOTS

    block = ctx.enter_context(nc.Block())

    @block.sync
    def _(sp):
        sp.dma_start(x_nat[:], x[0].rearrange("(t p) d -> p t d", p=P)).then_inc(x_in, 16)
        sp.dma_start(const[:], table).then_inc(early_in, 16)
        sp.dma_start(w_ab[:], w_in_v[:, :, COL["ab"]:COL["ab"] + 16]).then_inc(early_in, 16)
        sp.dma_start(conv_rows[:], dn_conv_w[0].rearrange("j (c p) -> (j c) p", p=P)).then_inc(early_in, 16)
        sp.dma_start(dtb[:], dn_dt_bias[0:1, :].to_broadcast([P, H])).then_inc(vec_in, 16)
        sp.dma_start(alog[:], dn_a_log[0:1, :].to_broadcast([P, H])).then_inc(vec_in, 16)
        sp.dma_start(normw[:], dn_norm_w[0].rearrange("(p a) -> p a", a=1)).then_inc(vec_in, 16)

        def load(phase, i, b):
            for k, src in enumerate(tiles_of(phase, i * 2 + b)):
                sp.dma_start(mixw[:, b, k], src).then_inc(mix_in[b][k], 16)

        for b in range(2):
            load(0, 0, b)

        def load_weights(names, pair, b):
            for n in names:
                w = (w_gate_e, w_up_e, w_down_e)[n]
                for a in range(2):
                    src = w[0, bass.ds(pair * 2 + a, 1)].rearrange("a (p k) n -> p (a k n)", p=P)
                    sp.dma_start(ring[:, 6 * b + 3 * a + n], src).then_inc(exp_in[6 * b + 3 * a + n], 16)

        for phase in range(3):
            with sp.Fori(1 if phase == 0 else 0, H // 2) as i:
                for b in range(2):
                    sp.wait_ge(proj_done, (i * 2 + (phase * H + b - 1)) * 4)
                    sp.sem_inc(load_turn, 1)
                    load(phase, i, b)
            if phase == 0:
                sp.wait_ge(ab_set, 1)
                sp.wait_ge(xT_vec, 3)
                sp.wait_ge(gate_vec, 1)
                load_weights(range(3), 0, 0)
                sp.wait_ge(scan_mm, SCAN_MM)
                sp.dma_start(ln1v[:, 0], ln1_g[0:1, :].to_broadcast([P, D])).then_inc(ln1_in, 16)
                sp.dma_start(ln1v[:, 1], ln1_b[0:1, :].to_broadcast([P, D])).then_inc(ln1_in, 16)
            if phase == 1:
                sp.wait_ge(rms_vec, 8)
                load_weights(range(3), 1, 1)
                sp.dma_start(w_rout[:], w_router[0].rearrange("(k p) n -> p k n", p=P)).then_inc(rout_in, 16)
                sp.dma_start(r_bias[:], router_bias[0:1, :].to_broadcast([P, NE])).then_inc(rout_in, 16)
        sp.wait_ge(proj_done, 4 * (3 * H - 1))
        sp.dma_start(w_gu_s[:, 0], w_gate_s[0].rearrange("(k p) n -> p k n", p=P)).then_inc(shared_in[0], 16)
        sp.dma_start(w_gu_s[:, 1], w_up_s[0].rearrange("(k p) n -> p k n", p=P)).then_inc(shared_in[1], 16)
        sp.wait_ge(proj_done, 4 * 3 * H)
        sp.dma_start(w_d_s[:], w_down_s[0].rearrange("(c p) n -> p c n", p=P)).then_inc(shared_in[2], 16)
        sp.dma_start(ln2v[:, 0], ln2_g[0:1, :].to_broadcast([P, D])).then_inc(ln2_in, 16)
        sp.dma_start(ln2v[:, 1], ln2_b[0:1, :].to_broadcast([P, D])).then_inc(ln2_in, 16)

        def stream(first_pair, i):
            for b in range(2):
                j = first_pair + i * 2 + b
                sp.wait_ge(gu_done, j)
                sp.sem_inc(load_turn, 1)
                load_weights((0, 1), i * 2 + b, b)
                sp.wait_ge(down_done, j - 1)
                sp.sem_inc(load_turn, 1)
                load_weights((2,), i * 2 + b, b)

        with sp.Fori(1, PAIRS // 2) as i:
            stream(0, i)
        sp.wait_ge(rout_step, ROUT_MOST)
        with sp.If(sp.value_load(most_i[0:1, 0:1], min_val=0, max_val=T) > SLOTS):
            with sp.Fori(1, PASSES) as q:
                with sp.Fori(0, PAIRS // 2) as i:
                    stream(q * PAIRS, i)
        sp.wait_ge(ln2_vec, LN_VEC)
        sp.dma_start(out[0].rearrange("(t p) d -> p t d", p=P), x_nat[:]).then_inc(out_sent, 16)
        sp.wait_ge(out_sent, 16)

    @block.tensor
    def _(pe):
        mm, tr = nc.tensor.matmul, nc.tensor.transpose
        pe.sem_inc(v_turned, 1)
        pe.sem_inc(pair_done, 2)
        pe.sem_inc(att_mm, 3)
        pe.sem_inc(gu_done, 1)
        pe.sem_inc(scat_done, 1)
        pe.sem_inc(inv_mm, 12)
        pe.wait_ge(x_in, 16)
        pe.wait_ge(early_in, 48)
        for b in range(4):
            for n in range(4):
                k, t = 2 * b + n // 2, n % 2
                last = tr(bank[b][:, n * P:(n + 1) * P], x_nat[:, t, k * P:(k + 1) * P], ident)
            last.then_inc(x_turned, 1)
        tr(bank[4][:, 0:96], conv_rows[:], ident[0:96, 0:96]).then_inc(x_turned, 1)
        pe.wait_ge(xT_vec, 2)
        pe.wait_ge(xT_act, 2)
        for k in range(KC):
            last = mm(bank[5][0:16, 0:T], w_ab[:, k, :], xT[:, k, :], start=(k == 0), stop=(k == KC - 1))
        last.then_inc(ab_done, 1)
        pe.wait_ge(ab_set, 1)
        for t in range(TT):
            last = tr(bank[6][:, t * 16:(t + 1) * 16], abT[:, t * P:(t + 1) * P], ident[0:16, 0:16])
        last.then_inc(ab_done, 1)
        pe.wait_ge(const_set, 6)
        pe.wait_ge(gate_vec, GATE_G)
        flat_g = decay_g[:].rearrange("p t h -> p (t h)")
        mm(bank[7][:, 0:16], c("tri"), flat_g, start=True, stop=True)
        mm(bank[7][:, 16:32], ones[:], flat_g, start=True, stop=True).then_inc(cum_done, 1)
        pe.wait_ge(gate_vec, GATE_WIDE)
        for n in range(TT * H):
            last = mm(bank[n // 4][:, (n % 4) * P:(n % 4 + 1) * P], g_wide[:, n], c("tri"), start=True, stop=True)
            if n % 4 == 3:
                last.then_inc(wide_done, 1)

        def project(phase, i, b, k, dst, rhs=xT, natural=False):
            pe.wait_ge(mix_in[b][k], i * 16 + (phase * H // 2 + 1) * 16)
            for t in range(TT if natural else 1):
                for kc in range(KC):
                    if natural:
                        last = mm(dst[:, t * P:(t + 1) * P], rhs[:, kc, t * P:(t + 1) * P], mixw[:, b, k, kc],
                                  start=(kc == 0), stop=(kc == KC - 1))
                    else:
                        last = mm(dst[:, 0:T], mixw[:, b, k, kc], rhs[:, kc, :],
                                  start=(kc == 0), stop=(kc == KC - 1))
            last.then_inc(proj_done, 1)

        pe.wait_ge(dist_done, DIST_BANKS)
        with pe.Fori(0, H // 2) as i:
            for b in range(2):
                h = i * 2 + b
                for n in range(3):
                    pe.wait_ge(conv_step, h * 12 + 4 * (n + 1))
                    project(0, i, b, n, bank[n])
                pe.wait_ge(act_done, h * 4 + 4)
                project(0, i, b, 3, bank[3])
                pe.wait_ge(act_done, h * 4 + 7)
                pe.wait_ge(vb_done, h * 2 + 2)
                for t in range(TT):
                    last = tr(bank[6][:, t * P:(t + 1) * P], v_act[:, t * P:(t + 1) * P], ident)
                last.then_inc(v_turned, 1)
        with pe.Fori(0, H // 2) as i:
            for b in range(2):
                h = i * 2 + b
                pe.wait_ge(sq_done, h + 1)
                pe.wait_ge(norm_act, h * 2 + 2)
                mm(bank[b][:], ones[:], sq[:, b], start=True, stop=True).then_inc(sumsq_done, 1)
            for b in range(2):
                h = i * 2 + b
                pe.wait_ge(norm_set, h + 3)
                pe.wait_ge(pair_set, h * 6 + 6)
                pe.wait_ge(kd_set, h + 1)
                for t in range(TT):
                    both = kn[:, b].rearrange("p (a t c) -> p a t c", a=2, t=TT)[:, :, t, :]
                    mm(bank[2 + b][:, t * 2 * P:(t + 1) * 2 * P], kn[:, b, t * P:(t + 1) * P], both,
                       start=True, stop=True)
                tr(bank[4 + b][:, 0:P], kn[:, b, 0:P], ident).then_inc(pair_done, 1)

        def group(t, g, q):
            return t[:, g // 2, 4 * (g % 2) + q]

        for g in range(4):
            pe.wait_ge(masked, g + 1)
            for q in range(4):
                last = tr(bank[g][:, q * P:(q + 1) * P], group(LM, g, q), ident)
            last.then_inc(lm_turned, 1)
        with pe.Fori(0, LEVELS - 1) as j:
            for g in range(4):
                pe.wait_ge(masked, j * 4 + (5 + g))
                pe.wait_ge(inv_vec, j * 4 + (5 + g))
                pe.wait_ge(inv_act, j * 8 + (5 + g))
                for q in range(4):
                    last = mm(bank[g][:, q * P:(q + 1) * P], group(LM, g, q), group(U, g, q), start=True, stop=True)
                last.then_inc(inv_mm, 1)
            for g in range(4):
                pe.wait_ge(inv_act, j * 8 + (9 + g))
                for q in range(4):
                    last = mm(bank[4 + g][:, q * P:(q + 1) * P], group(TI, g, q), group(W, g, q),
                              start=True, stop=True)
                last.then_inc(inv_mm, 1)
            for g in range(4):
                pe.wait_ge(inv_vec, j * 4 + (9 + g))
                for q in range(4):
                    last = tr(bank[g][:, q * P:(q + 1) * P], group(U, g, q), ident)
                last.then_inc(inv_mm, 1)

        def heads(f, dst, n):
            for q in range(4):
                last = f(4 * n + q, dst[:, q * P:(q + 1) * P])
            last.then_inc(scan_mm, 1)

        pe.wait_ge(inv_act, 8 * LEVELS)
        pe.wait_ge(vb_done, 2 + 2 * H)
        for n in range(2):
            heads(lambda h, o: mm(o, U[:, 0, h], vb[:, 0, h], start=True, stop=True), bank[n], n)
        pe.wait_ge(kd_set, 2 + H)
        for n in range(2):
            pe.wait_ge(scan_act, n + 1)
            heads(lambda h, o: mm(o, kd0[:, h], V[:, 0, h], start=True, stop=True), bank[2 + n], n)
        for n in range(2):
            heads(lambda h, o: mm(o, V[:, 0, h], AT[:, 0, h], start=True, stop=True), bank[4 + n], n)
        for n in range(2):
            pe.wait_ge(scan_act, n + 3)
            heads(lambda h, o: mm(o, kT1[:, h], S1[:, h], start=True, stop=True), bank[6 + n], n)
        for n in range(2):
            pe.wait_ge(scan_vec, 2 + 4 * (n + 1))
            heads(lambda h, o: mm(o, U[:, 1, h], R[:, h], start=True, stop=True), bank[n], n)

        def second_out(h, o):
            mm(o, S1[:, h], qd1[:, h], start=True, stop=False)
            return mm(o, V[:, 1, h], AT[:, 1, h], start=False, stop=True)

        for n in range(2):
            pe.wait_ge(scan_act, n + 5)
            heads(second_out, bank[2 + n], n)
        for n in range(4):
            pe.wait_ge(rms_act, n + 1)
            pe.wait_ge(scan_vec, 10 if n >= 2 else 2)
            mm(bank[4 + n][:], ones[:], osq[:, 2 * n:2 * n + 2].rearrange("p a t -> p (a t)"),
               start=True, stop=True).then_inc(rms_mm, 1)

        pe.wait_ge(scan_vec, 12)
        pe.wait_ge(rms_act, 8)
        with pe.Fori(0, H // 2) as i:
            for b in range(2):
                h = i * 2 + b
                pe.wait_ge(att_act, h * 8 + 8)
                project(1, i, b, 0, bank[0])
                project(1, i, b, 1, bank[1])
                project(1, i, b, 2, bank[2], natural=True)
                pe.wait_ge(att_act, h * 8 + 10)
                pe.wait_ge(att_vec, h * 9 + 1)
                mm(bank[4][:, 0:P], qkT[:, 0, 0:P], qkT[:, 1, 0:P], start=True, stop=True)
                mm(bank[4][:, P:3 * P], qkT[:, 0, P:T], qkT[:, 1, :], start=True, stop=True).then_inc(att_mm, 1)
                project(1, i, b, 3, bank[3])
                pe.wait_ge(att_vec, h * 9 + 16)
                for n in range(3):
                    last = tr(bank[5][:, n * P:(n + 1) * P], prob[:, n], ident)
                last.then_inc(att_mm, 1)
                pe.wait_ge(att_act, h * 8 + 15)
                mm(bank[6][:, 0:P], v_nat[:, 0], probT[:, 0], start=True, stop=True)
                mm(bank[6][:, P:T], v_nat[:, 0], probT[:, 1], start=True, stop=False)
                mm(bank[6][:, P:T], v_nat[:, 1], probT[:, 2], start=False, stop=True).then_inc(att_mm, 1)

        pe.wait_ge(att_act, 8 + 8 * H)
        pe.wait_ge(rms_vec, 8)
        pe.wait_ge(const_set, 7)
        for n in range(4):
            mm(bank[4 + n][:], zeros[:, 0:P], zeros[:], start=True, stop=False, skip_group_check=True)
        with pe.Fori(0, H // 2) as i:
            for b in range(2):
                h = i * 2 + b
                pe.wait_ge(mer_act, h + 1)
                project(2, i, b, 0, bank[0])
                pe.wait_ge(mer_vec, h * 5 + 3)
                project(2, i, b, 1, bank[1], rhs=szT)
                pe.wait_ge(mer_vec, h * 5 + 5)
                project(2, i, b, 2, bank[2], rhs=yaT)
                pe.wait_ge(mer_vec, h * 5 + 10)
                pe.wait_ge(mix_in[b][3], i * 16 + (H + 1) * 16)
                wide = mixw[:, b, 3].rearrange("p k c -> p (k c)")
                for t in range(TT):
                    for s in range(2):
                        last = mm(bank[4 + 2 * t + s][:], merged[:, b, t * P:(t + 1) * P],
                                  wide[:, s * 512:(s + 1) * 512], start=False, stop=False, skip_group_check=True)
                last.then_inc(proj_done, 1)

        for b in range(4):
            pe.wait_ge(ln_vec, LN_VEC if b == 0 else LN_VEC)
            for n in range(4):
                k, t = 2 * b + n // 2, n % 2
                last = tr(bank[b][:, n * P:(n + 1) * P], x_nat[:, t, k * P:(k + 1) * P], ident)
            last.then_inc(x1_turned, 1)
        pe.wait_ge(x1T_vec, 2)
        pe.wait_ge(x1T_act, 2)
        pe.wait_ge(rout_in, 32)
        for k in range(KC):
            last = mm(bank[0][0:NE, 0:T], w_rout[:, k], x1T[:, k], start=(k == 0), stop=(k == KC - 1))
        last.then_inc(log_done, 1)

        def shared(n, dst):
            pe.wait_ge(shared_in[n], 16)
            for f in range(2):
                for k in range(KC):
                    last = mm(dst[:, f * T:(f + 1) * T], w_gu_s[:, n, k, f * P:(f + 1) * P], x1T[:, k],
                              start=(k == 0), stop=(k == KC - 1))
            last.then_inc(sh_done, 1)

        shared(0, bank[3])
        pe.wait_ge(logT_set, 1)
        for t in range(TT):
            last = tr(bank[1][:, t * NE:(t + 1) * NE], logT[:, t * P:(t + 1) * P], ident[0:NE, 0:NE])
        last.then_inc(log_turned, 1)
        shared(1, bank[0])
        pe.wait_ge(rout_step, ROUT_SEL)
        mm(bank[2][:, 0:NE], c("before"), selm[:, 0], start=True, stop=True)
        mm(bank[2][:, NE:2 * NE], c("before"), selm[:, 1], start=True, stop=False)
        mm(bank[2][:, NE:2 * NE], ones[:], selm[:, 0], start=False, stop=True)
        mm(bank[2][:, 2 * NE:3 * NE], ones[:], selm[:, 0], start=True, stop=False)
        mm(bank[2][:, 2 * NE:3 * NE], ones[:], selm[:, 1], start=False, stop=True).then_inc(pos_done, 1)
        pe.wait_ge(hsT_set, 1)
        pe.wait_ge(shared_in[2], 16)
        for t in range(TT):
            for n in range(2):
                for f in range(2):
                    last = mm(bank[4 + 2 * t + n][:], hsT[:, f, t * P:(t + 1) * P], w_d_s[:, f, n * 512:(n + 1) * 512],
                              start=(f == 0), stop=False, skip_group_check=True)
        last.then_inc(shd_done, 1)

        def gather(step):
            for c2 in range(2):
                k = 2 * step + c2
                for n in range(4):
                    last = mm(bank[3][:, c2 * 256:(c2 + 1) * 256], x1r[:, n // 2, n % 2, k], pick[:, n // 2],
                              start=(n == 0), stop=(n == 3))
            last.then_inc(gath_done, 1)

        def scatter(b, part):
            for n in part:
                t, s, half = n // 4, n // 2 % 2, n % 2
                last = mm(bank[4 + 2 * t + s][:], drop[:, b, t * P:(t + 1) * P], yr[:, half, s * 512:(s + 1) * 512],
                          start=False, stop=False, skip_group_check=True)
            return last

        def expert_pass(q):
            for step in range(4):
                pe.wait_ge(pick_set, q * 72 + 2)
                if step == 0:
                    pe.wait_ge(hidT_set, q * PAIRS + 1)
                else:
                    pe.wait_ge(xg_set, q * 68 + step)
                gather(step)
            with pe.Fori(0, NE // 8) as i:
                for m in range(4):
                    b, n = m % 2, i * 2 + m // 2
                    j = q * PAIRS + (i * 4 + m)
                    slot = 6 * b
                    for a in range(2):
                        for w in range(2):
                            pe.wait_ge(exp_in[slot + 3 * a + w], q * 256 + i * 32 + (m // 2) * 16 + 16)
                    pe.wait_ge(xg_set, q * 68 + n * 4 + 4)
                    pe.wait_ge(hid_set, j + 1)
                    tokens = xg[m // 2][:, b]
                    for k in range(KC):
                        for a in range(2):
                            last = mm(bank[0][64 * a:64 * a + 64, :], tokens[:, k, 64 * a:64 * a + 64],
                                      ring[:, slot + 3 * a:slot + 3 * a + 2, k * FE:(k + 1) * FE],
                                      start=(k == 0), stop=(k == KC - 1))
                        if k == 1:
                            pe.wait_ge(pick_set, q * 72 + n * 4 + 6)
                            pe.wait_ge(hidT_set, j + 1)
                            gather(2 * b)
                        if k == 4:
                            pe.wait_ge(xg_set, q * 68 + n * 4 + (5 + 2 * b))
                            gather(2 * b + 1)
                        if k == 6:
                            pe.wait_ge(xg_set, q * 68 + n * 4 + (6 + 2 * b))
                            for t in range(TT):
                                turned = tr(bank[3][:, t * P:(t + 1) * P],
                                            wpick[:, m // 2, t, b * P:(b + 1) * P], ident)
                            turned.then_inc(wp_turned, 1)
                    last.then_inc(gu_done, 1)
                    pe.wait_ge(ylo_set, j * 2 + 2)
                    pe.wait_ge(drop_set, j * 2 + 2)
                    scatter(1 - b, range(6))
                    pe.wait_ge(hid_set, j + 2)
                    pe.wait_ge(drop_set, j * 2 + 4)
                    for f in range(2):
                        last = tr(bank[3][:, f * P:(f + 1) * P], hid[:, f], ident)
                    last.then_inc(hid_turned, 1)
                    scatter(1 - b, range(6, 8)).then_inc(scat_done, 1)
                    pe.wait_ge(hidT_set, j + 2)
                    for a in range(2):
                        pe.wait_ge(exp_in[slot + 3 * a + 2], q * 256 + i * 32 + (m // 2) * 16 + 16)
                    for s in range(2):
                        for f in range(2):
                            for a in range(2):
                                last = mm(bank[1 + s][64 * a:64 * a + 64, :], hidT[:, f, 64 * a:64 * a + 64],
                                          ring[:, slot + 3 * a + 2, f * D + s * 512:f * D + (s + 1) * 512],
                                          start=(f == 0), stop=(f == 1))
                    last.then_inc(down_done, 1)

        def last_pair(passes):
            pe.wait_ge(ylo_set, passes * PAIRS * 2 + 2)
            pe.wait_ge(drop_set, passes * PAIRS * 2 + 2)
            scatter(1, range(8)).then_inc(acc_done, 1)

        pe.wait_ge(clear_set, 2)
        pe.wait_ge(x1hi_set, 2)
        pe.wait_ge(x1lo_set, 2)
        pe.wait_ge(gsh_set, 1)
        expert_pass(0)
        with pe.If(pe.value_load(most_i[0:1, 0:1], min_val=0, max_val=T) > SLOTS):
            with pe.Fori(1, PASSES) as q:
                expert_pass(q)
            last_pair(PASSES)
        with pe.Else():
            last_pair(1)

    @block.scalar
    def _(act):
        A = nc.scalar.activation
        act.sem_inc(act_done, 4)
        act.sem_inc(vb_done, 2)
        act.sem_inc(norm_act, 4)
        act.sem_inc(kd_set, 2)
        act.sem_inc(inv_act, 8)
        act.sem_inc(att_act, 8)
        act.sem_inc(mer_act, 1)
        act.sem_inc(hidT_set, 1)
        nc.scalar.preload_act_table_set("natural_log_exp_and_others")
        for b in (1, 3):
            act.wait_ge(x_turned, b + 1)
            A(xT[:, 2 * b:2 * b + 2].rearrange("p k t -> p (k t)"), bank[b][:], ACT.Copy).then_inc(xT_act, 1)
        act.wait_ge(vec_in, 48)
        act.wait_ge(gate_vec, 3)
        s = Steps(act, gate_act)
        s.then(A(g_e[:, :, 0:H], g_abs[:], ACT.Exp, scale=-1.0))
        act.wait_ge(const_set, 6)
        s.did(A(g_e[:, :, 0:H], g_e[:, :, 0:H], ACT.Ln, bias=one[:]))
        s.did(A(alog[:], alog[:], ACT.Exp))
        s.did(A(g_e[:, :, H:16], ab[:, :, H:16], ACT.Exp, scale=-1.0))
        act.wait_ge(gate_vec, GATE_CUM)
        s.did(A(e_last[:], e_last[:], ACT.Exp))
        s.did(A(nbeg[:], gcl[:, 0], ACT.Exp))
        for n in range(TT * H):
            act.wait_ge(wide_done, n // 4 + 1)
            A(edist[:, n], bank[n // 4][:, (n % 4) * P:(n % 4 + 1) * P], ACT.Abs,
              bias=ngc[:, n:n + 1]).then_inc(dist_done, 1)
        for n in range(2):
            A(qd1[:, 4 * n:4 * n + 4].rearrange("p h c -> p (h c)"), bank[2 + n][:], ACT.Exp).then_inc(dist_done, 1)
        act.wait_ge(dist_done, 18)
        A(edist[:], edist[:], ACT.Exp, scale=-1.0).then_inc(dist_done, 1)

        nc.scalar.preload_act_table_set("silu_and_others")
        act.wait_ge(gate_vec, GATE_ALL)
        with act.Fori(0, H // 2) as i:
            for b in range(2):
                h = i * 2 + b
                for n in range(2):
                    act.wait_ge(conv_step, h * 12 + (12 + 4 * (n + 1)))
                    A(kq[:, bass.ds(h, 1), n * T:(n + 1) * T].rearrange("p a t -> p (a t)"), acc[:, n],
                      ACT.Silu).then_inc(act_done, 1)
                act.wait_ge(conv_step, h * 12 + 24)
                act.wait_ge(v_turned, h + 1)
                A(v_act[:], acc[:, 2], ACT.Silu).then_inc(act_done, 1)
                act.wait_ge(proj_done, h * 4 + 4)
                A(szT[:, bass.ds(h, 1)].rearrange("p a t -> p (a t)"), bank[3][:, 0:T], ACT.Silu).then_inc(act_done, 1)
                act.wait_ge(v_turned, h + 2)
                for t in range(TT):
                    A(vb[:, t, bass.ds(h, 1)].rearrange("p a c -> p (a c)"), bank[6][:, t * P:(t + 1) * P], ACT.Copy,
                      scale=beta[:, t, bass.ds(h, 1)]).then_inc(vb_done, 1)

        nc.scalar.preload_act_table_set("natural_log_exp_and_others")
        act.wait_ge(act_done, 4 + 4 * H)
        with act.Fori(0, H // 2) as i:
            for b in range(2):
                A(sq[:, b], kq[:, bass.ds(i * 2 + b, 1)].rearrange("p a t -> p (a t)"), ACT.Square).then_inc(sq_done, 1)
            for b in range(2):
                h = i * 2 + b
                act.wait_ge(sumsq_done, h + 1)
                act.wait_ge(norm_set, h + 1)
                A(rr[:, b], bank[b][:], ACT.Ln, bias=eps_l2[:]).then_inc(norm_act, 1)
                act.wait_ge(norm_act, h * 2 + 5)
                A(rr[:, b], rr[:, b], ACT.Exp, scale=-0.5).then_inc(norm_act, 1)
            for b in range(2):
                h = i * 2 + b
                act.wait_ge(pair_done, h + 3)
                A(kd0[:, bass.ds(h, 1)].rearrange("p a c -> p (a c)"), bank[4 + b][:, 0:P], ACT.Copy,
                  scale=e_last[:, bass.ds(h, 1)]).then_inc(kd_set, 1)

        def rows(t, g):
            return t[:, g // 2, 4 * (g % 2):4 * (g % 2) + 4].rearrange("p h c -> p (h c)")

        with act.Fori(0, LEVELS - 1) as j:
            for g in range(4):
                act.wait_ge(inv_mm, j * 12 + (13 + g))
                A(rows(W, g), bank[g][:], ACT.Copy).then_inc(inv_act, 1)
            for g in range(4):
                act.wait_ge(inv_mm, j * 12 + (21 + g))
                A(rows(TI, g), bank[g][:], ACT.Copy).then_inc(inv_act, 1)

        def four(t, n):
            return t[:, 4 * n:4 * n + 4].rearrange("p h c -> p (h c)")

        for n in range(2):
            act.wait_ge(scan_mm, n + 1)
            A(four(V[:, 0], n), bank[n][:], ACT.Copy).then_inc(scan_act, 1)
        for n in range(2):
            act.wait_ge(scan_mm, n + 3)
            A(four(S1, n), bank[2 + n][:], ACT.Copy).then_inc(scan_act, 1)
        for n in range(2):
            act.wait_ge(scan_mm, n + 9)
            A(four(V[:, 1], n), bank[n][:], ACT.Copy).then_inc(scan_act, 1)
        act.wait_ge(scan_mm, SCAN_MM)
        act.wait_ge(scan_vec, 12)
        def pair(t, n):
            return t[:, 2 * n:2 * n + 2].rearrange("p h t -> p (h t)")

        for n in range(4):
            A(pair(osq, n), pair(oT, n), ACT.Square).then_inc(rms_act, 1)
        for n in range(4):
            act.wait_ge(rms_mm, n + 1)
            A(pair(osq, n), bank[4 + n][:], ACT.Ln, scale=1.0 / DH, bias=eps_rms[:]).then_inc(rms_act, 1)
        act.wait_ge(rms_act, 8)
        for n in range(4):
            A(pair(osq, n), pair(osq, n), ACT.Exp, scale=-0.5).then_inc(rms_act, 1)

        nc.scalar.preload_act_table_set("exp_and_others")
        with act.Fori(0, H // 2) as i:
            for b in range(2):
                h = i * 2 + b
                act.wait_ge(att_mm, h * 3 + 1)
                for n in range(2):
                    act.wait_ge(proj_done, h * 4 + (4 * H + 1 + n))
                    A(qkT[:, n], bank[n][:, 0:T], ACT.Copy).then_inc(att_act, 1)
                act.wait_ge(att_mm, h * 3 + 3)
                act.wait_ge(proj_done, h * 4 + (4 * H + 3))
                A(v_nat[:].rearrange("p t c -> p (t c)"), bank[2][:, 0:T], ACT.Copy).then_inc(att_act, 1)
                act.wait_ge(att_vec, h * 9 + 13)
                A(prob[:, 0], score[:, 0], ACT.Exp, bias=smx[:, 2:3], accum_out=smx[:, 4:5]).then_inc(att_act, 1)
                A(prob[:, 1:3].rearrange("p a c -> p (a c)"), score[:, 1:3].rearrange("p a c -> p (a c)"), ACT.Exp,
                  bias=smx[:, 3:4], accum_out=smx[:, 5:6]).then_inc(att_act, 1)
                act.wait_ge(proj_done, h * 4 + (4 * H + 4))
                act.wait_ge(att_vec, h * 9 + 9)
                A(gtmp[:, 0], bank[3][:, 0:T], ACT.Exp, scale=-1.0).then_inc(att_act, 1)
                act.wait_ge(att_mm, h * 3 + 5)
                A(probT[:].rearrange("p a c -> p (a c)"), bank[5][:, 0:3 * P], ACT.Copy).then_inc(att_act, 1)
                act.wait_ge(att_mm, h * 3 + 6)
                A(yaT[:, bass.ds(h, 1)].rearrange("p a t -> p (a t)"), bank[6][:, 0:T], ACT.Copy).then_inc(att_act, 1)

        act.wait_ge(att_vec, 9 + 9 * H)
        with act.Fori(0, H // 2) as i:
            for b in range(2):
                h = i * 2 + b
                act.wait_ge(proj_done, h * 4 + (8 * H + 1))
                act.wait_ge(mer_vec, h * 5 + 3)
                A(gtmp[:, 0], bank[0][:, 0:T], ACT.Exp, scale=-1.0).then_inc(mer_act, 1)

        nc.scalar.preload_act_table_set("natural_log_exp_and_others")
        for t in range(TT):
            act.wait_ge(ln_vec, 8 * t + 5)
            A(moment[:, t, 1:2], moment[:, t, 1:2], ACT.Ln, bias=eps_ln[:]).then_inc(ln_act, 1)
            act.wait_ge(ln_act, 2 * t + 1)
            A(moment[:, t, 1:2], moment[:, t, 1:2], ACT.Exp, scale=-0.5).then_inc(ln_act, 1)

        nc.scalar.preload_act_table_set("sigmoid_and_others")
        for b in (1, 3):
            act.wait_ge(x1_turned, b + 1)
            A(x1T[:, 2 * b:2 * b + 2].rearrange("p k t -> p (k t)"), bank[b][:], ACT.Copy).then_inc(x1T_act, 1)
        act.wait_ge(log_done, 1)
        A(logT[:], bank[0][0:NE, 0:T], ACT.Copy).then_inc(logT_set, 1)
        for t in range(TT):
            A(x1r[:, t, 0].rearrange("p k q -> p q k"), x_nat[:, t].rearrange("p (q k) -> p q k", k=KC),
              ACT.Copy).then_inc(x1hi_set, 1)
        act.wait_ge(log_turned, 1)
        A(sco[:].rearrange("p t e -> p (t e)"), bank[1][:, 0:2 * NE], ACT.Sigmoid).then_inc(sco_set, 1)
        nc.scalar.preload_act_table_set("silu_and_others")
        act.wait_ge(sh_done, 1)
        A(gsh[:], bank[3][:], ACT.Silu).then_inc(gsh_set, 1)

        def evacuate(q, n, step, buffer):
            act.wait_ge(gath_done, q * 68 + n * 4 + (step + 1))
            A(xg[buffer][:, :, 2 * step:2 * step + 2].rearrange("p a k s -> p k a s"),
              bank[3][:].rearrange("p (k a s) -> p k a s", k=2, a=2), ACT.Copy).then_inc(xg_set, 1)

        def expert_pass(q):
            act.wait_ge(gu_done, q * PAIRS + 1)
            for step in range(4):
                evacuate(q, 0, step, 0)
            with act.Fori(0, NE // 8) as i:
                for m in range(4):
                    b, n = m % 2, i * 2 + m // 2
                    j = q * PAIRS + (i * 4 + m)
                    act.wait_ge(gu_done, j + (1 - b))
                    evacuate(q, n + 1, 2 * b, 1 - m // 2)
                    evacuate(q, n + 1, 2 * b + 1, 1 - m // 2)
                    act.wait_ge(gu_done, j + 2)
                    act.wait_ge(hid_set, j + 1)
                    A(gact[:], bank[0][:, 0:FE], ACT.Silu).then_inc(act_set, 1)
                    act.wait_ge(hid_turned, j + 1)
                    A(hidT[:].rearrange("p f s -> p (f s)"), bank[3][:, 0:2 * P], ACT.Copy).then_inc(hidT_set, 1)
                    act.wait_ge(down_done, j + 1)
                    act.wait_ge(drop_set, j * 2 + 4)
                    for s in range(2):
                        A(yr[:, 0, s * 512:(s + 1) * 512], bank[1 + s][:], ACT.Copy,
                          scale=wslot[:, b:b + 1]).then_inc(yhi_set, 1)

        expert_pass(0)
        with act.If(act.value_load(most_i[0:1, 0:1], min_val=0, max_val=T) > SLOTS):
            with act.Fori(1, PASSES) as q:
                expert_pass(q)

        nc.scalar.preload_act_table_set("natural_log_exp_and_others")
        for t in range(TT):
            act.wait_ge(ln2_vec, 8 * t + 5)
            A(moment[:, t, 1:2], moment[:, t, 1:2], ACT.Ln, bias=eps_ln[:]).then_inc(ln2_act, 1)
            act.wait_ge(ln2_act, 2 * t + 1)
            A(moment[:, t, 1:2], moment[:, t, 1:2], ACT.Exp, scale=-0.5).then_inc(ln2_act, 1)

    @block.vector
    def _(dve):
        v = nc.vector
        dve.sem_inc(conv_step, 12)
        dve.sem_inc(norm_set, 2)
        dve.sem_inc(pair_set, 12)
        dve.sem_inc(att_vec, 9)
        dve.sem_inc(mer_vec, 5)
        dve.sem_inc(hid_set, 1)
        dve.sem_inc(ylo_set, 2)
        dve.sem_inc(drop_set, 2)
        for t, value in ((ones[:], 1.0), (one[:], 1.0), (eps_l2[:], L2_EPS), (eps_rms[:], RMS_EPS),
                         (eps_ln[:], LN_EPS), (smx[:], 0.0)):
            v.memset(t, value).then_inc(const_set, 1)
        for b in (0, 2):
            dve.wait_ge(x_turned, b + 1)
            v.tensor_copy(xT[:, 2 * b:2 * b + 2].rearrange("p k t -> p (k t)"), bank[b][:]).then_inc(xT_vec, 1)
        dve.wait_ge(x_turned, 5)
        v.tensor_copy(conv_w[:], bank[4][:, 0:96]).then_inc(xT_vec, 1)
        dve.wait_ge(ab_done, 1)
        v.tensor_copy(abT[:], bank[5][0:16, 0:T]).then_inc(ab_set, 1)
        s = Steps(dve, gate_vec)
        dve.wait_ge(ab_done, 2)
        s.then(v.tensor_copy(ab[:].rearrange("p t n -> p (t n)"), bank[6][:, 0:32]))
        dve.wait_ge(vec_in, 48)
        per_head = [P, TT, H]
        s.then(v.tensor_tensor(g_u[:], ab[:, :, 0:H], dtb[:].unsqueeze(1).to_broadcast(per_head), ALU.add))
        s.then(v.scalar_tensor_tensor(g_abs[:], g_u[:], -1.0, g_u[:], ALU.mult, ALU.max))
        dve.wait_ge(gate_act, 4)
        s.then(v.scalar_tensor_tensor(g_u[:], g_u[:], 0.0, g_e[:, :, 0:H], ALU.max, ALU.add))
        s.then(v.scalar_tensor_tensor(decay_g[:], g_u[:], -1.0, alog[:].unsqueeze(1).to_broadcast(per_head),
                                      ALU.mult, ALU.mult))
        assert s.count == GATE_G
        s.did(v.tensor_copy(g_wide[:], decay_g[:].rearrange("p t h -> p (t h)").unsqueeze(2).to_broadcast(
            [P, TT * H, P])))
        assert s.count == GATE_WIDE
        s.then(v.tensor_scalar(beta[:], g_e[:, :, H:16], 1.0, None, ALU.add))
        s.then(v.reciprocal(beta[:], beta[:]))
        dve.wait_ge(cum_done, 1)
        s.then(v.tensor_copy(gcl[:].rearrange("p a n -> p (a n)"), bank[7][:, 0:32]))
        s.did(v.tensor_scalar(ngc[:], gcl[:, 0], -1.0, None, ALU.mult))
        s.did(v.tensor_tensor(e_last[:], gcl[:, 1], gcl[:, 0], ALU.subtract))
        assert s.count == GATE_CUM
        dve.wait_ge(gate_act, 6)
        s.did(v.scalar_tensor_tensor(nbeg[:], nbeg[:], -1.0, beta[:].rearrange("p t h -> p (t h)"),
                                     ALU.mult, ALU.mult))
        dve.wait_ge(dist_done, 19)
        wide = [P, TT * H, P]
        s.did(v.scalar_tensor_tensor(AT[:].rearrange("p t h c -> p (t h) c"), edist[:], QK_SCALE,
                                     c("tri").unsqueeze(1).to_broadcast(wide), ALU.mult, ALU.mult))
        s.did(v.tensor_tensor(L[:].rearrange("p t h c -> p (t h) c"), edist[:],
                              c("strict").unsqueeze(1).to_broadcast(wide), ALU.mult))
        assert s.count == GATE_ALL

        dve.wait_ge(xT_vec, 3)
        s = Steps(dve, conv_step)
        s.count = 12
        with dve.Fori(0, H // 2) as i:
            s.enter(i, 24)
            for b in range(2):
                h = i * 2 + b
                for n, first in enumerate((8, 0, 16)):
                    def tap(j):
                        return conv_w[:, bass.ds(h + (j * 24 + first), 1)]
                    dve.wait_ge(proj_done, h * 4 + (n + 1))
                    dve.wait_ge(act_done, h * 4 + (n + 1))
                    s.then(v.tensor_scalar(acc[:, n], bank[n][:, 0:T], tap(3), None, ALU.mult))
                    for d in range(1, 4):
                        f = s.then if d < 3 else s.did
                        f(v.scalar_tensor_tensor(acc[:, n, d:T], bank[n][:, 0:T - d], tap(3 - d), acc[:, n, d:T],
                                                 ALU.mult, ALU.add))
            s.leave(H // 2)

        def row(t, h):
            return t[:, bass.ds(h, 1)].rearrange("p a c -> p (a c)")

        dve.wait_ge(v_turned, 1 + H)
        with dve.Fori(0, H // 2) as i:
            for b in range(2):
                h = i * 2 + b
                dve.wait_ge(norm_act, h * 2 + 6)
                dve.wait_ge(pair_done, h + 1)
                dve.wait_ge(pair_set, h * 6 + 6)
                v.tensor_tensor(kn[:, b], row(kq, h), rr[:, b], ALU.mult).then_inc(norm_set, 1)
            for b in range(2):
                h = i * 2 + b
                dve.wait_ge(norm_set, h + 3)
                dve.wait_ge(pair_done, h + 3)
                for t in range(TT):
                    both = bank[2 + b][:, t * 2 * P:(t + 1) * 2 * P]
                    v.scalar_tensor_tensor(row(L[:, t], h), both[:, 0:P], beta[:, t, bass.ds(h, 1)],
                                           row(L[:, t], h), ALU.mult, ALU.mult).then_inc(pair_set, 1)
                    v.tensor_tensor(row(AT[:, t], h), both[:, P:2 * P], row(AT[:, t], h),
                                    ALU.mult).then_inc(pair_set, 1)
                v.tensor_copy(row(kT1, h), kn[:, b, P:T]).then_inc(pair_set, 1)
                v.scalar_tensor_tensor(row(qd1, h), kn[:, b, T + P:2 * T], QK_SCALE, row(qd1, h),
                                       ALU.mult, ALU.mult).then_inc(pair_set, 1)

        def heads(t, g):
            return t[:, g // 2, 4 * (g % 2):4 * (g % 2) + 4]

        four = [P, 4, P]
        levels = c("levels", LEVELS)
        dve.wait_ge(pair_set, 12 + 6 * H)
        dve.wait_ge(act_done, 4 + 4 * H)
        for g in range(4):
            v.tensor_tensor(heads(LM, g), heads(L, g), levels[:, 0].unsqueeze(1).to_broadcast(four),
                            ALU.mult).then_inc(masked, 1)
        eye = ident.unsqueeze(1).to_broadcast(four)
        dve.wait_ge(masked, 4)
        for g in range(4):
            v.tensor_tensor(heads(TI, g), eye, heads(LM, g), ALU.subtract).then_inc(inv_vec, 1)
        for g in range(4):
            dve.wait_ge(lm_turned, g + 1)
            v.tensor_tensor(heads(U, g), eye, bank[g][:].rearrange("p (h c) -> p h c", h=4),
                            ALU.subtract).then_inc(inv_vec, 1)
        dve.wait_ge(inv_vec, 8)
        with dve.Fori(0, LEVELS - 1) as j:
            for g in range(4):
                dve.wait_ge(inv_mm, j * 12 + (1 + g))
                v.tensor_tensor(heads(LM, g), heads(L, g),
                                levels[:, bass.ds(j + 1, 1)].to_broadcast(four), ALU.mult).then_inc(masked, 1)
            for g in range(4):
                dve.wait_ge(inv_mm, j * 12 + (17 + g))
                v.tensor_tensor(heads(U, g), heads(U, g), bank[4 + g][:].rearrange("p (h c) -> p h c", h=4),
                                ALU.subtract).then_inc(inv_vec, 1)

        for n in range(2):
            dve.wait_ge(scan_mm, n + 5)
            v.tensor_copy(oT[:, 4 * n:4 * n + 4, 0:P], bank[4 + n][:].rearrange("p (h c) -> p h c", h=4)).then_inc(
                scan_vec, 1)
        for h in range(H):
            dve.wait_ge(scan_mm, h // 4 + 7)
            v.scalar_tensor_tensor(R[:, h], bank[6 + h // 4][:, (h % 4) * P:(h % 4 + 1) * P],
                                   nbeg[:, H + h:H + h + 1], vb[:, 1, h], ALU.mult, ALU.add).then_inc(scan_vec, 1)
        for n in range(2):
            dve.wait_ge(scan_mm, n + 11)
            v.tensor_copy(oT[:, 4 * n:4 * n + 4, P:T], bank[2 + n][:].rearrange("p (h c) -> p h c", h=4)).then_inc(
                scan_vec, 1)
        dve.wait_ge(scan_vec, 10)
        v.memset(zeros[:], 0.0).then_inc(const_set, 1)
        def pair(t, n):
            return t[:, 2 * n:2 * n + 2].rearrange("p h t -> p (h t)")

        for n in range(4):
            dve.wait_ge(rms_act, 9 + n)
            v.tensor_tensor(pair(oT, n), pair(oT, n), pair(osq, n), ALU.mult).then_inc(rms_vec, 1)
        for n in range(4):
            dve.wait_ge(rms_vec, n + 1)
            v.scalar_tensor_tensor(pair(szT, n), pair(oT, n), normw[:], pair(szT, n), ALU.mult,
                                   ALU.mult).then_inc(rms_vec, 1)

        s = Steps(dve, att_vec)
        s.count = 9
        with dve.Fori(0, H // 2) as i:
            s.enter(i, 18)
            for b in range(2):
                h = i * 2 + b
                dve.wait_ge(att_mm, h * 3 + 4)
                dve.wait_ge(att_act, h * 8 + 5)
                s.then(v.scalar_tensor_tensor(score[:].rearrange("p a c -> p (a c)"), bank[4][:, 0:3 * P], QK_SCALE,
                                              c("causal"), ALU.mult, ALU.add))
                s.did(v.tensor_reduce(smx[:, 0:1], score[:, 0], AX.X, ALU.max))
                s.then(v.tensor_reduce(smx[:, 1:2], score[:, 1:3].rearrange("p a c -> p (a c)"), AX.X, ALU.max))
                s.did(v.tensor_scalar(smx[:, 2:4], smx[:, 0:2], -1.0, None, ALU.mult))
                dve.wait_ge(att_act, h * 8 + 13)
                s.then(v.reciprocal(smx[:, 6:8], smx[:, 4:6]))
                s.did(v.tensor_scalar(prob[:, 0], prob[:, 0], smx[:, 6:7], None, ALU.mult))
                flat = prob[:, 1:3].rearrange("p a c -> p (a c)")
                s.did(v.tensor_scalar(flat, flat, smx[:, 7:8], None, ALU.mult))
                dve.wait_ge(att_act, h * 8 + 14)
                s.then(v.tensor_scalar(gtmp[:, 0], gtmp[:, 0], 1.0, None, ALU.add))
                s.did(v.reciprocal(row(sga, h), gtmp[:, 0]))
            s.leave(H // 2)

        s2 = Steps(dve, mer_vec)
        s2.count = 5
        s.settle()
        with dve.Fori(0, H // 2) as i:
            s2.enter(i, 10)
            for b in range(2):
                h = i * 2 + b
                dve.wait_ge(mer_act, h + 2)
                s2.then(v.tensor_scalar(gtmp[:, 0], gtmp[:, 0], 1.0, None, ALU.add))
                s2.then(v.reciprocal(gtmp[:, 0], gtmp[:, 0]))
                dve.wait_ge(proj_done, h * 4 + (8 * H + 2))
                s2.did(v.tensor_tensor(gtmp[:, 1], bank[1][:, 0:T], gtmp[:, 0], ALU.mult))
                dve.wait_ge(proj_done, h * 4 + (8 * H + 3))
                s2.then(v.tensor_tensor(merged[:, b], bank[2][:, 0:T], row(sga, h), ALU.mult))
                s2.did(v.tensor_tensor(merged[:, b], merged[:, b], gtmp[:, 1], ALU.add))
            s2.leave(H // 2)

        def layer_norm(done, act_sem, gb):
            s = Steps(dve, done)
            for t in range(TT):
                for n in range(2):
                    half = x_nat[:, t, n * 512:(n + 1) * 512]
                    s.then(v.scalar_tensor_tensor(half, half, ALPHA, bank[4 + 2 * t + n][:], ALU.mult, ALU.add))
                for n in range(2):
                    s.did(v.bn_stats(stats[:, t, n], x_nat[:, t, n * 512:(n + 1) * 512]))
                s.settle()
                s.then(v.bn_aggr(moment[:, t], stats[:, t].rearrange("p n s -> p (n s)")))
                dve.wait_ge(act_sem, 2 * t + 2)
                s.then(v.tensor_scalar(x_nat[:, t], x_nat[:, t], moment[:, t, 0:1], moment[:, t, 1:2],
                                       ALU.subtract, ALU.mult))
                s.then(v.tensor_tensor(x_nat[:, t], x_nat[:, t], gb[:, 0], ALU.mult))
                s.then(v.tensor_tensor(x_nat[:, t], x_nat[:, t], gb[:, 1], ALU.add))
            assert s.count == LN_VEC

        dve.wait_ge(proj_done, 12 * H)
        dve.wait_ge(ln1_in, 32)
        layer_norm(ln_vec, ln_act, ln1v)

        for b in (0, 2):
            dve.wait_ge(x1_turned, b + 1)
            v.tensor_copy(x1T[:, 2 * b:2 * b + 2].rearrange("p k t -> p (k t)"), bank[b][:]).then_inc(x1T_vec, 1)
        for t in range(TT):
            dve.wait_ge(x1hi_set, t + 1)
            v.tensor_tensor(x1r[:, t, 1].rearrange("p k q -> p q k"), x_nat[:, t].rearrange("p (q k) -> p q k", k=KC),
                            x1r[:, t, 0].bitcast(F32).rearrange("p k q -> p q k"), ALU.subtract).then_inc(x1lo_set, 1)

        s = Steps(dve, rout_step)
        dve.wait_ge(sco_set, 1)
        dve.wait_ge(rout_in, 32)
        all_e, grouped = [P, TT, NE], [P, TT, GROUPS, NE // GROUPS]
        s.then(v.tensor_tensor(cho[:], sco[:], r_bias[:].unsqueeze(1).to_broadcast(all_e), ALU.add))
        for t in range(TT):
            for g in range(GROUPS):
                s.did(v.max(best[:, t, g], cho[:, t, g * 8:(g + 1) * 8]))
        s.settle()
        s.then(v.tensor_tensor(gsc[:], best[:, :, :, 0], best[:, :, :, 1], ALU.add))
        own, other = gsc[:].unsqueeze(3).to_broadcast([P, TT, 8, 8]), gsc[:].unsqueeze(2).to_broadcast([P, TT, 8, 8])
        s.did(v.tensor_tensor(cmp1[:], other, own, ALU.is_gt))
        s.then(v.tensor_tensor(cmp2[:], other, own, ALU.is_equal))
        tie = c("tie", GROUPS).unsqueeze(1).to_broadcast([P, TT, 8, 8])
        s.then(v.tensor_tensor(cmp2[:], cmp2[:], tie, ALU.mult))
        s.then(v.tensor_tensor(cmp1[:], cmp1[:], cmp2[:], ALU.add))
        s.then(v.tensor_reduce(gmk[:], cmp1[:], AX.X, ALU.add))
        s.then(v.tensor_scalar(gmk[:], gmk[:], TOP_G - 0.5, None, ALU.is_lt))
        s.did(v.tensor_scalar(goff[:], gmk[:], 1.0, -NEG, ALU.subtract, ALU.mult))
        by_group = cho[:].rearrange("p t (g e) -> p t g e", g=GROUPS)
        s.then(v.tensor_tensor(by_group, by_group, gmk[:].unsqueeze(3).to_broadcast(grouped), ALU.mult))
        s.then(v.tensor_tensor(by_group, by_group, goff[:].unsqueeze(3).to_broadcast(grouped), ALU.add))
        for t in range(TT):
            s.did(v.max(top[:, t], cho[:, t]))
        s.settle()
        for t in range(TT):
            s.did(v.match_replace(rep_[:, t], top[:, t], cho[:, t], 4 * NEG))
        s.settle()
        s.then(v.tensor_tensor(selm[:], rep_[:], cho[:], ALU.not_equal))
        assert s.count == ROUT_SEL, s.count
        s.then(v.tensor_tensor(sco[:], sco[:], selm[:], ALU.mult))
        s.then(v.tensor_reduce(wsum[:], sco[:], AX.X, ALU.add))
        s.then(v.reciprocal(wsum[:], wsum[:]))
        dve.wait_ge(pos_done, 1)
        s.then(v.tensor_reduce(most[:], bank[2][:, 2 * NE:3 * NE], AX.X, ALU.max))
        s.did(v.tensor_copy(most_i[:], most[:]))
        assert s.count == ROUT_MOST, s.count
        s.did(v.memset(pos[:], -1.0))
        s.then(v.memset(wgt[:], 0.0))
        for t in range(TT):
            s.did(v.tensor_scalar(wgt[:, t, 0:NE], sco[:, t], wsum[:, t:t + 1], ROUTED_SCALE, ALU.mult, ALU.mult))
        places = pos[:, :, 0:NE]
        s.then(v.scalar_tensor_tensor(places, bank[2][:, 0:2 * NE].rearrange("p (t e) -> p t e", t=TT), 1.0, selm[:],
                                      ALU.add, ALU.mult))
        s.then(v.tensor_scalar(places, places, 1.0, None, ALU.subtract))
        dve.wait_ge(gsh_set, 1)
        dve.wait_ge(sh_done, 2)
        v.tensor_tensor(hsT[:].rearrange("p f t -> p (f t)"), bank[0][:], gsh[:], ALU.mult).then_inc(hsT_set, 1)
        dve.wait_ge(shd_done, 1)
        v.memset(yr[:].bitcast(F32), 0.0).then_inc(clear_set, 1)
        v.memset(drop[:].bitcast(F32), 0.0).then_inc(clear_set, 1)

        def places_of(first, buffer, before):
            spread = [P, BATCH, SLOTS]
            slots = c("slot").unsqueeze(1).to_broadcast(spread)
            for t in range(TT):
                v.tensor_tensor(pick[:, t].rearrange("p (e s) -> p e s", e=BATCH),
                                pos[:, t, bass.ds(first, BATCH)].unsqueeze(2).to_broadcast(spread), slots,
                                ALU.is_equal).then_inc(pick_set, 1)
            dve.wait_ge(pick_set, before + 2)
            for t in range(TT):
                v.tensor_tensor(wpick[:, buffer, t].rearrange("p (e s) -> p e s", e=BATCH),
                                pick[:, t].bitcast(F32).rearrange("p (e s) -> p e s", e=BATCH),
                                wgt[:, t, bass.ds(first, BATCH)].unsqueeze(2).to_broadcast(spread),
                                ALU.mult).then_inc(pick_set, 1)

        def expert_pass(q):
            places_of(0, 0, q * 72)
            dve.wait_ge(gath_done, q * 68 + 4)
            dve.wait_ge(pick_set, q * 72 + 4)
            places_of(BATCH, 1, q * 72 + 4)
            with dve.Fori(0, NE // 8) as i:
                for m in range(4):
                    b, n = m % 2, i * 2 + m // 2
                    j = q * PAIRS + (i * 4 + m)
                    dve.wait_ge(wp_turned, j + 1)
                    dve.wait_ge(scat_done, j + 1)
                    v.tensor_scalar(drop[:, b], bank[3][:, 0:T], 0.0, None, ALU.is_gt).then_inc(drop_set, 1)
                    v.tensor_reduce(wslot[:, b:b + 1], bank[3][:, 0:T], AX.X, ALU.add).then_inc(drop_set, 1)
                    dve.wait_ge(act_set, j + 1)
                    v.tensor_tensor(hid[:].rearrange("p f s -> p s f"), gact[:].rearrange("p (s f) -> p s f", f=2),
                                    bank[0][:, FE:2 * FE].rearrange("p (s f) -> p s f", f=2),
                                    ALU.mult).then_inc(hid_set, 1)
                    if b == 1:
                        dve.wait_ge(gath_done, q * 68 + n * 4 + 8)
                        dve.wait_ge(pick_set, q * 72 + n * 4 + 8)
                        places_of(n * BATCH + 2 * BATCH, m // 2, q * 72 + n * 4 + 8)
                    for s in range(2):
                        dve.wait_ge(yhi_set, j * 2 + (s + 1))
                        part = slice(s * 512, (s + 1) * 512)
                        v.scalar_tensor_tensor(yr[:, 1, part], bank[1 + s][:], wslot[:, b:b + 1],
                                               yr[:, 0, part].bitcast(F32), ALU.mult,
                                               ALU.subtract).then_inc(ylo_set, 1)

        s.settle()
        expert_pass(0)
        with dve.If(dve.value_load(most_i[0:1, 0:1], min_val=0, max_val=T) > SLOTS):
            with dve.Fori(1, PASSES) as q:
                dve.wait_ge(pick_set, q * 72)
                v.tensor_scalar(pos[:], pos[:], float(SLOTS), None, ALU.subtract).then_inc(rout_step, 1)
                dve.wait_ge(rout_step, q + s.count)
                expert_pass(q)

        dve.wait_ge(acc_done, 1)
        dve.wait_ge(ln2_in, 32)
        layer_norm(ln2_vec, ln2_act, ln2v)


_INS = ["x", "w_in", "dn_conv_w", "dn_a_log", "dn_dt_bias", "dn_norm_w", "w_branch_a", "w_branch_b", "w_out", "ln1_g",
        "ln1_b", "w_router", "router_bias", "w_gate_e", "w_up_e", "w_down_e", "w_gate_s", "w_up_s", "w_down_s",
        "ln2_g", "ln2_b"]


def kernel(**inputs):
    import concourse.bacc as bacc
    from concourse.bass_utils import run_bass_kernel_spmd

    nc = bacc.Bacc("TRN2", target_bir_lowering=False, num_devices=1)
    arrays = {f"in_{name}": np.ascontiguousarray(inputs[name]) for name in _INS}
    arrays["in_table"] = constants()
    args = [nc.dram_tensor(name, a.shape, mybir.dt.from_np(a.dtype), kind="ExternalInput").ap()
            for name, a in arrays.items()]
    out = nc.dram_tensor("out", inputs["x"].shape, F32, kind="ExternalOutput").ap()
    program(nc, *args, out)
    return run_bass_kernel_spmd(nc, [arrays], core_ids=[0]).results[0]["out"]
```

```python
from contextlib import ExitStack

import numpy as np

import concourse.bass as bass
from concourse import mybir

F32 = mybir.dt.float32
F32R = mybir.dt.float32r
I32 = mybir.dt.int32
BF16 = mybir.dt.bfloat16
ALU = mybir.AluOpType
ACT = mybir.ActivationFunctionType
AX = mybir.AxisListType

P = 128
D = 1024
T = 256
TT = T // P
KC = D // P
H = 8
DH = 128
NE = 64
FE = 256
GROUPS = 8
TOP_G = 4
SLOTS = 64
LEVELS = 7
ALPHA = 2 ** 0.25
LN_EPS = 1e-5
RMS_EPS = 1e-6
L2_EPS = 1e-6
ROUTED_SCALE = 2.5
QK_SCALE = DH ** -0.5
NEG = -1e30

COL = {}
_at = 0
for _name, _n in (("qa", 1024), ("ka", 1024), ("va", 1024), ("qb", 1024), ("kb", 1024), ("vb", 1024), ("z", 1024),
                  ("ab", 16), ("ga", 1024), ("gb", 1024)):
    COL[_name] = _at
    _at += _n

CONST = {}
_at = 0
for _name, _n in (("ident", P), ("tri", P), ("before", P), ("strict", P), ("levels", LEVELS * P),
                  ("causal", 3 * P), ("slot", SLOTS), ("tie", GROUPS * GROUPS)):
    CONST[_name] = (_at, _at + _n)
    _at += _n
NCONST = _at


def constants():
    c = np.zeros((P, NCONST), np.float32)
    r = np.arange(P)
    def put(name, a):
        c[:, CONST[name][0]:CONST[name][1]] = a
    put("ident", np.eye(P))
    put("tri", r[:, None] <= r[None, :])
    put("before", r[:, None] < r[None, :])
    put("strict", r[:, None] > r[None, :])
    levels = []
    for s in range(LEVELS):
        b = 1 << s
        same = (r[:, None] // (2 * b)) == (r[None, :] // (2 * b))
        levels.append(same & ((r[:, None] // b) % 2 == 1) & ((r[None, :] // b) % 2 == 0))
    put("levels", np.concatenate(levels, 1))
    diag = np.where(r[None, :] <= r[:, None], 0.0, NEG)
    put("causal", np.concatenate([diag, np.zeros((P, P)), diag], 1))
    put("slot", np.arange(SLOTS)[None, :])
    g = np.arange(GROUPS)
    put("tie", (g[None, :] < g[:, None]).astype(np.float32).reshape(1, -1))
    return c


class Steps:

    def __init__(self, engine, semaphore):
        self.engine, self.semaphore = engine, semaphore
        self.count, self.trip = 0, None

    def did(self, instruction):
        instruction.then_inc(self.semaphore, 1)
        self.count += 1

    def settle(self):
        value = self.count
        if self.trip is not None:
            value = self.trip[0] * self.trip[1] + self.count
        self.engine.wait_ge(self.semaphore, value)

    def then(self, instruction):
        self.did(instruction)
        self.settle()

    def enter(self, i, per):
        self.trip, self.start = (i, per), self.count

    def leave(self, trips):
        per = self.trip[1]
        assert self.count - self.start == per, (self.count - self.start, per)
        self.count, self.trip = self.start + trips * per, None


def program(nc, x, w_in, dn_conv_w, dn_a_log, dn_dt_bias, dn_norm_w, w_branch_a, w_branch_b, w_out, ln1_g, ln1_b,
            w_router, router_bias, w_gate_e, w_up_e, w_down_e, w_gate_s, w_up_s, w_down_s, ln2_g, ln2_b, table, out):
    with ExitStack() as ctx:
        build(nc, ctx, x, w_in, dn_conv_w, dn_a_log, dn_dt_bias, dn_norm_w, w_branch_a, w_branch_b, w_out, ln1_g,
              ln1_b, w_router, router_bias, w_gate_e, w_up_e, w_down_e, w_gate_s, w_up_s, w_down_s, ln2_g, ln2_b,
              table, out)


def build(nc, ctx, x, w_in, dn_conv_w, dn_a_log, dn_dt_bias, dn_norm_w, w_branch_a, w_branch_b, w_out, ln1_g, ln1_b,
          w_router, router_bias, w_gate_e, w_up_e, w_down_e, w_gate_s, w_up_s, w_down_s, ln2_g, ln2_b, table, out):
    def sem(name):
        return ctx.enter_context(nc.semaphore(name))

    place = {}

    def at(name, shape, offset, dtype=F32):
        t = nc.alloc_sbuf_tensor_at(name, shape, dtype, offset=offset)
        place[name] = offset + -(-int(np.prod(shape[1:])) * (2 if dtype == BF16 else 4) // 32) * 32
        return t

    SLOT = 2048
    RING = 16512
    MIXW = RING + 12 * SLOT * 4
    REST = MIXW + 32768
    ring = at("ring", [P, 12, SLOT], RING)
    mixw = at("mixw", [P, 2, 4, KC, P], MIXW)
    xhi = at("xhi", [P, KC, T], RING, F32R)
    xlo = at("xlo", [P, KC, T], place["xhi"], F32R)
    whi = at("whi", [P, 4, KC, P], place["xlo"], F32R)
    wlo = at("wlo", [P, 4, KC, P], place["whi"], F32R)
    x_nat = at("x_nat", [P, TT, D], REST)
    xT = at("xT", [P, KC, T], place["x_nat"])
    const = at("const", [P, NCONST], place["xT"])
    sga = at("sga", [P, KC, T], place["const"])
    yahi = at("yahi", [P, H, T], place["sga"], F32R)
    szT = at("szT", [P, H, T], place["yahi"])
    kT1 = at("kT1", [P, H, P], place["szT"])
    qd1 = at("qd1", [P, H, P], place["kT1"])
    kd0 = at("kd0", [P, H, P], place["qd1"])
    vb = at("vb", [P, TT, H, DH], place["kd0"])
    TEMP = place["vb"]
    acc = at("acc", [P, 3, T], TEMP)
    v_act = at("v_act", [P, T], place["acc"])
    conv_rows = at("conv_rows", [96, P], place["szT"])
    w_ab = at("w_ab", [P, KC, 16], place["conv_rows"])
    kn = at("kn", [P, 2, 2 * T], TEMP)
    qkT = at("qkT", [P, 2, T], TEMP)
    v_nat = at("v_nat", [P, TT, DH], place["qkT"])
    score = at("score", [P, 3, P], place["v_nat"])
    prob = at("prob", [P, 3, P], place["score"])
    probT = at("probT", [P, 3, P], place["prob"])
    gtmp = at("gtmp", [P, 2, T], place["probT"])
    vT = at("vT", [P, T], place["probT"] + T * 4)
    merged = at("merged", [P, T], TEMP)
    mhi = at("mhi", [P, 2, T], place["merged"], F32R)
    mlo = at("mlo", [P, 2, T], place["mhi"], F32R)
    assert place["mlo"] <= place["probT"]
    SMALL = max(place["v_act"], place["gtmp"])
    conv_w = at("conv_w", [P, 96], SMALL)
    abT = at("abT", [16, T], place["w_ab"])
    szhi = at("szhi", [P, H, T], place["x_nat"], F32R)
    szlo = at("szlo", [P, H, T], place["kd0"], F32R)
    yalo = at("yalo", [P, H, T], RING + 11 * SLOT * 4, F32R)
    ab = at("ab", [P, TT, 16], place["conv_w"])
    dtb = at("dtb", [P, H], place["ab"])
    alog = at("alog", [P, H], place["dtb"])
    normw = at("normw", [P, 1], place["alog"])
    g_u = at("g_u", [P, TT, H], place["normw"])
    g_abs = at("g_abs", [P, TT, H], place["g_u"])
    g_e = at("g_e", [P, TT, 16], place["g_abs"])
    decay_g = at("decay_g", [P, TT, H], place["g_e"])
    beta = at("beta", [P, TT, H], place["decay_g"])
    gcl = at("gcl", [P, 2, TT * H], place["beta"])
    ngc = at("ngc", [P, TT * H], place["gcl"])
    e_last = at("e_last", [P, TT * H], place["ngc"])
    nbeg = at("nbeg", [P, TT * H], place["e_last"])
    smx = at("smx", [P, 8], place["nbeg"])
    eps_l2 = at("eps_l2", [P, 1], place["smx"])
    eps_rms = at("eps_rms", [P, 1], place["eps_l2"])
    one = at("one", [P, 1], place["eps_rms"])
    eps_ln = at("eps_ln", [P, 1], place["one"])
    ones = at("ones", [P, P], place["eps_ln"])
    stats = at("stats", [P, TT, 2, 6], place["ones"])
    moment = at("moment", [P, TT, 2], place["stats"])
    END = place["moment"]
    assert END <= nc.sbuf_usable_end, (END, nc.sbuf_usable_end)
    L = at("L", [P, TT, H, P], RING + 6 * SLOT * 4)
    AT = at("AT", [P, TT, H, P], place["L"])
    LM = at("LM", [P, TT, H, P], place["AT"])
    W = at("W", [P, TT, H, P], place["LM"])
    U = at("U", [P, TT, H, P], place["W"])
    TI = at("TI", [P, TT, H, P], place["U"])
    kq = at("kq", [P, H, 2 * T], place["AT"])
    R = at("R", [P, H, DH], place["AT"])
    osq = at("osq", [P, H, T], place["AT"])
    oT = at("oT", [P, H, T], place["LM"])
    V = at("V", [P, TT, H, DH], place["U"])
    S1 = at("S1", [P, H, DH], place["AT"] + 4096)
    sq = at("sq", [P, 2, 2 * T], place["W"])
    rr = at("rr", [P, 2, 2 * T], place["W"] + 4096)
    g_wide = at("g_wide", [P, TT * H, P], place["U"])
    edist = at("edist", [P, TT * H, P], place["W"])

    def c(name, n=None):
        a = const[:, CONST[name][0]:CONST[name][1]]
        return a if n is None else a.rearrange("p (n c) -> p n c", n=n)

    ident = c("ident")

    bank = [ctx.enter_context(nc.psum_tensor(f"bank{i}", [P, 512], F32)) for i in range(8)]

    x_in, early_in, vec_in, ln1_in = sem("x_in"), sem("early_in"), sem("vec_in"), sem("ln1_in")
    mix_in = [[sem(f"mix_in{b}{k}") for k in range(4)] for b in range(2)]
    const_set = sem("const_set")
    x_turned, xT_vec, xhi_set, xlo_set = sem("x_turned"), sem("xT_vec"), sem("xhi_set"), sem("xlo_set")
    whi_set, wlo_set = sem("whi_set"), [sem("wlo_even_set"), sem("wlo_odd_set")]
    ab_done, ab_set = sem("ab_done"), sem("ab_set")
    gate_vec, gate_act = sem("gate_vec"), sem("gate_act")
    cum_done, wide_done, dist_done = sem("cum_done"), sem("wide_done"), sem("dist_done")
    proj_done = sem("proj_done")
    conv_step, act_done = sem("conv_step"), sem("act_done")
    v_turned, vb_done = sem("v_turned"), sem("vb_done")
    sq_done, sumsq_done, norm_act, norm_set = sem("sq_done"), sem("sumsq_done"), sem("norm_act"), sem("norm_set")
    pair_done, pair_set, kd_set = sem("pair_done"), sem("pair_set"), sem("kd_set")
    masked, lm_turned = sem("masked"), sem("lm_turned")
    inv_mm, inv_act, inv_vec = sem("inv_mm"), sem("inv_act"), sem("inv_vec")
    scan_mm, scan_act, scan_vec = sem("scan_mm"), sem("scan_act"), sem("scan_vec")
    rms_act, rms_vec, rms_mm = sem("rms_act"), sem("rms_vec"), sem("rms_mm")
    score_done, att_vec = sem("score_done"), sem("att_vec")
    vT_turned, p_turned, pv_done = sem("vT_turned"), sem("p_turned"), sem("pv_done")
    qk_set, vT_set, exp_set, ga_set = sem("qk_set"), sem("vT_set"), sem("exp_set"), sem("ga_set")
    v_set, probT_set, yahi_set, yalo_set = sem("v_set"), sem("probT_set"), sem("yahi_set"), sem("yalo_set")
    szhi_set, szlo_set = sem("szhi_set"), sem("szlo_set")
    gb_set, mer_vec, mhi_set, mlo_set = sem("gb_set"), sem("mer_vec"), sem("mhi_set"), sem("mlo_set")
    ln_act, ln_vec = sem("ln_act"), sem("ln_vec")
    out_sent = sem("out_sent")
    load_turn = sem("load_turn")
    rout_in, shared_in, ln2_in = sem("rout_in"), [sem("gate_s_in"), sem("up_s_in"), sem("down_s_in")], sem("ln2_in")
    exp_in = [sem(f"exp_in{n}") for n in range(12)]
    x1_turned, x1T_vec, x1T_act = sem("x1_turned"), sem("x1T_vec"), sem("x1T_act")
    x1hi_set, x1lo_set = sem("x1hi_set"), sem("x1lo_set")
    log_done, logT_set, log_turned, sco_set = sem("log_done"), sem("logT_set"), sem("log_turned"), sem("sco_set")
    mixed = sem("mixed")
    rout_step, pos_done = sem("rout_step"), sem("pos_done")
    sh_done, gsh_set, hsT_set = sem("sh_done"), sem("gsh_set"), sem("hsT_set")
    clear_set, pick_set, gath_done, xg_set = sem("clear_set"), sem("pick_set"), sem("gath_done"), sem("xg_set")
    gu_done, act_set, hid_set = sem("gu_done"), sem("act_set"), sem("hid_set")
    hid_turned, hidT_set, down_done = sem("hid_turned"), sem("hidT_set"), sem("down_done")
    yhi_set, ylo_set, wp_turned, drop_set = sem("yhi_set"), sem("ylo_set"), sem("wp_turned"), sem("drop_set")
    scat_done, acc_done = sem("scat_done"), sem("acc_done")
    ln2_act, ln2_vec = sem("ln2_act"), sem("ln2_vec")

    w_in_v = w_in[0].rearrange("(k p) n -> p k n", p=P)
    wa_v = w_branch_a[0].rearrange("(k p) n -> p k n", p=P)
    wb_v = w_branch_b[0].rearrange("(k p) n -> p k n", p=P)
    wo_v = w_out[0].rearrange("(k p) n -> p k n", p=P)
    PAIRS, BATCH = NE // 2, 4
    x1r = at("x1r", [P, TT, 2, KC, P], place["const"], F32R)
    yr = at("yr", [P, 2, D], place["x1r"], F32R)
    xg0 = at("xg0", [P, 2, KC, P], place["szT"])
    w_rout = at("w_rout", [P, KC, NE], place["qd1"])
    r_bias = at("r_bias", [P, NE], place["w_rout"])
    zeros = at("zeros", [P, 512], place["r_bias"], BF16)
    pos = at("pos", [P, TT, NE + 2 * BATCH], place["r_bias"])
    wgt = at("wgt", [P, TT, NE + 2 * BATCH], place["pos"])
    xg1 = at("xg1", [P, 2, KC, P], place["kd0"])
    xg = [xg0, xg1]
    pick = at("pick", [P, TT, BATCH * SLOTS], TEMP, F32R)
    wpick = at("wpick", [P, 2, TT, BATCH * SLOTS], place["pick"])
    drop = at("drop", [P, 2, T], place["wpick"], F32R)
    x1T = at("x1T", [P, KC, T], place["x_nat"])
    hid = at("hid", [P, 2, P], place["x_nat"])
    hidT = at("hidT", [P, 2, P], place["hid"])
    gact = at("gact", [P, FE], place["hidT"])
    wslot = at("wslot", [P, 2], place["gact"])
    gsh = at("gsh", [P, 2 * T], place["xT"] + CONST["levels"][0] * 4)
    hsT = at("hsT", [P, 2, T], place["gsh"])
    w_gu_s = at("w_gu_s", [P, 2, KC, FE], MIXW)
    w_d_s = at("w_d_s", [P, 2, D], place["w_gu_s"])
    ln2v = at("ln2v", [P, 2, D], place["w_d_s"])
    logT = at("logT", [NE, T], place["kd0"])
    sco = at("sco", [P, TT, NE], place["logT"])
    cho = at("cho", [P, TT, NE], place["sco"])
    rep_ = at("rep_", [P, TT, NE], place["cho"])
    selm = at("selm", [P, TT, NE], place["rep_"])
    best = at("best", [P, TT, GROUPS, 8], place["selm"])
    gsc = at("gsc", [P, TT, GROUPS], place["best"])
    gmk = at("gmk", [P, TT, GROUPS], place["gsc"])
    goff = at("goff", [P, TT, GROUPS], place["gmk"])
    cmp1 = at("cmp1", [P, TT, GROUPS, GROUPS], place["goff"])
    cmp2 = at("cmp2", [P, TT, GROUPS, GROUPS], place["cmp1"])
    top = at("top", [P, TT, 8], place["cmp2"])
    wsum = at("wsum", [P, TT], place["top"])
    most = at("most", [P, 1], place["wsum"])
    most_i = at("most_i", [P, 1], SMALL, I32)
    ln1v = at("ln1v", [P, 2, D], place["szT"])

    def tile_of(phase, h, k):
        def w(name):
            return w_in_v[:, :, bass.ds(COL[name] + h * P, P)]
        if phase == 0:
            return w(("vb", "kb", "qb", "z")[k])
        if phase == 1:
            return w(("qa", "ka", "va", "ga")[k])
        if k == 0:
            return w("gb")
        if k == 1:
            before = 0 if isinstance(h, int) and h == 0 else h - 1
            return wo_v[:, bass.ds(before, 1), :].rearrange("p a (k c) -> p (a k) c", k=KC)
        return (wb_v if k == 2 else wa_v)[:, :, bass.ds(h * P, P)]

    GATE_G, GATE_WIDE, GATE_CUM, GATE_ALL = 5, 6, 11, 14
    DIST_BANKS, SCAN_MM, LN_STATS, LN_TILE = 18, 12, 5, 7
    ROUT_SEL, ROUT_MOST = 32, 37
    PASSES = T // SLOTS

    block = ctx.enter_context(nc.Block())

    @block.sync
    def _(sp):
        sp.dma_start(x_nat[:], x[0].rearrange("(t p) d -> p t d", p=P)).then_inc(x_in, 16)
        sp.dma_start(const[:], table).then_inc(early_in, 16)
        sp.dma_start(w_ab[:], w_in_v[:, :, COL["ab"]:COL["ab"] + 16]).then_inc(early_in, 16)
        sp.dma_start(conv_rows[:], dn_conv_w[0].rearrange("j (c p) -> (j c) p", p=P)).then_inc(early_in, 16)
        sp.dma_start(dtb[:], dn_dt_bias[0:1, :].to_broadcast([P, H])).then_inc(vec_in, 16)
        sp.dma_start(alog[:], dn_a_log[0:1, :].to_broadcast([P, H])).then_inc(vec_in, 16)
        sp.dma_start(normw[:], dn_norm_w[0].rearrange("(p a) -> p a", a=1)).then_inc(vec_in, 16)

        def load(phase, i, b):
            for k in range(4):
                sp.dma_start(mixw[:, b, k], tile_of(phase, i * 2 + b, k)).then_inc(mix_in[b][k], 16)

        def load_freed(phase, i, b):
            for w in wlo_set:
                sp.wait_ge(w, i * 4 + (16 * phase + 2 * b - 2))
            sp.sem_inc(load_turn, 1)
            load(phase, i, b)

        for b in range(2):
            load(0, 0, b)

        def load_expert(pair, b, parts):
            for n in parts:
                w = (w_gate_e, w_up_e, w_down_e)[n % 3]
                src = w[0, bass.ds(pair * 2 + n // 3, 1)].rearrange("a (p k) n -> p (a k n)", p=P)
                sp.dma_start(ring[:, 6 * b + n], src).then_inc(exp_in[6 * b + n], 16)

        for phase in range(3):
            if phase > 0:
                for b in range(2):
                    load_freed(phase, 0, b)
            if phase == 1:
                sp.wait_ge(scan_mm, SCAN_MM)
                sp.dma_start(ln1v[:, 0], ln1_g[0:1, :].to_broadcast([P, D])).then_inc(ln1_in, 16)
                sp.dma_start(ln1v[:, 1], ln1_b[0:1, :].to_broadcast([P, D])).then_inc(ln1_in, 16)
            with sp.Fori(1, H // 2) as i:
                for b in range(2):
                    load_freed(phase, i, b)
            if phase == 1:
                sp.wait_ge(rms_vec, 8)
                load_expert(1, 1, range(5))
                sp.dma_start(w_rout[:], w_router[0].rearrange("(k p) n -> p k n", p=P)).then_inc(rout_in, 16)
                sp.dma_start(r_bias[:], router_bias[0:1, :].to_broadcast([P, NE])).then_inc(rout_in, 16)
        sp.wait_ge(wlo_set[1], 2 * (3 * H - 1))
        sp.dma_start(mixw[:, 0, 1], tile_of(2, H, 1)).then_inc(mix_in[0][1], 16)
        sp.wait_ge(wlo_set[0], 2 * 3 * H)
        sp.wait_ge(wlo_set[1], 2 * 3 * H)
        sp.dma_start(w_d_s[:], w_down_s[0].rearrange("(c p) n -> p c n", p=P)).then_inc(shared_in[2], 16)
        sp.dma_start(ln2v[:, 0], ln2_g[0:1, :].to_broadcast([P, D])).then_inc(ln2_in, 16)
        sp.dma_start(ln2v[:, 1], ln2_b[0:1, :].to_broadcast([P, D])).then_inc(ln2_in, 16)
        sp.dma_start(w_gu_s[:, 1], w_up_s[0].rearrange("(k p) n -> p k n", p=P)).then_inc(shared_in[1], 16)
        sp.wait_ge(wlo_set[1], 2 * 3 * H + 1)
        sp.dma_start(w_gu_s[:, 0], w_gate_s[0].rearrange("(k p) n -> p k n", p=P)).then_inc(shared_in[0], 16)
        sp.wait_ge(mixed, TT)
        load_expert(0, 0, range(6))
        load_expert(1, 1, (5,))

        def stream(first_pair, i):
            for b in range(2):
                j = first_pair + i * 2 + b
                sp.wait_ge(gu_done, j)
                sp.sem_inc(load_turn, 1)
                load_expert(i * 2 + b, b, (0, 1, 3, 4))
                sp.wait_ge(down_done, j - 1)
                sp.sem_inc(load_turn, 1)
                load_expert(i * 2 + b, b, (2, 5))

        with sp.Fori(1, PAIRS // 2) as i:
            stream(0, i)
        sp.wait_ge(rout_step, ROUT_MOST)
        with sp.If(sp.value_load(most_i[0:1, 0:1], min_val=0, max_val=T) > SLOTS):
            with sp.Fori(1, PASSES) as q:
                with sp.Fori(0, PAIRS // 2) as i:
                    stream(q * PAIRS, i)
        for t in range(TT):
            sp.wait_ge(ln2_vec, LN_TILE * (t + 1))
            sp.dma_start(out[0, t * P:(t + 1) * P, :], x_nat[:, t]).then_inc(out_sent, 16)
        sp.wait_ge(out_sent, 16 * TT)

    @block.tensor
    def _(pe):
        mm, tr = nc.tensor.matmul, nc.tensor.transpose
        pe.sem_inc(v_turned, 1)
        pe.sem_inc(pair_done, 2)
        pe.sem_inc(gu_done, 1)
        pe.sem_inc(scat_done, 1)
        pe.sem_inc(inv_mm, 12)
        pe.wait_ge(x_in, 16)
        pe.wait_ge(early_in, 48)
        for b in range(4):
            for n in range(4):
                k, t = 2 * b + n // 2, n % 2
                last = tr(bank[b][:, n * P:(n + 1) * P], x_nat[:, t, k * P:(k + 1) * P], ident)
            last.then_inc(x_turned, 1)
        tr(bank[4][:, 0:96], conv_rows[:], ident[0:96, 0:96]).then_inc(x_turned, 1)
        pe.wait_ge(xT_vec, 4)
        for k in range(KC):
            last = mm(bank[5][0:16, 0:T], w_ab[:, k, :], xT[:, k, :], start=(k == 0), stop=(k == KC - 1))
        last.then_inc(ab_done, 1)
        pe.wait_ge(ab_set, 1)
        for t in range(TT):
            last = tr(bank[6][:, t * 16:(t + 1) * 16], abT[:, t * P:(t + 1) * P], ident[0:16, 0:16])
        last.then_inc(ab_done, 1)
        pe.wait_ge(const_set, 6)
        pe.wait_ge(gate_vec, GATE_G)
        flat_g = decay_g[:].rearrange("p t h -> p (t h)")
        mm(bank[7][:, 0:16], c("tri"), flat_g, start=True, stop=True)
        mm(bank[7][:, 16:32], ones[:], flat_g, start=True, stop=True).then_inc(cum_done, 1)
        pe.wait_ge(xT_vec, 5)
        pe.wait_ge(gate_vec, GATE_WIDE)
        for n in range(TT * H):
            last = mm(bank[n // 4][:, (n % 4) * P:(n % 4 + 1) * P], g_wide[:, n], c("tri"), start=True, stop=True)
            if n % 4 == 3:
                last.then_inc(wide_done, 1)

        def split_in(phase, i, b, k):
            pe.wait_ge(wlo_set[k % 2], i * 4 + (16 * phase + 2 * b + k // 2 + 1))

        def three(dst, left, right, start, stop):
            hi, lo = 0, 1
            for n, (l, r) in enumerate(((hi, hi), (hi, lo), (lo, hi))):
                last = mm(dst, left[l], right[r], start=start and n == 0, stop=stop and n == 2,
                          skip_group_check=True)
            return last

        def project(phase, i, b, k, dst, rhs=(xhi, xlo)):
            split_in(phase, i, b, k)
            for kc in range(KC):
                last = three(dst[:, 0:T], (whi[:, k, kc], wlo[:, k, kc]), (rhs[0][:, kc, :], rhs[1][:, kc, :]),
                             kc == 0, kc == KC - 1)
            last.then_inc(proj_done, 1)

        pe.wait_ge(dist_done, DIST_BANKS)
        pe.wait_ge(xlo_set, 4)
        with pe.Fori(0, H // 2) as i:
            for b in range(2):
                h = i * 2 + b
                for n in range(3):
                    pe.wait_ge(conv_step, h * 12 + 4 * (n + 1))
                    project(0, i, b, n, bank[n])
                pe.wait_ge(act_done, h * 4 + 5)
                pe.wait_ge(vb_done, h * 2 + 2)
                for t in range(TT):
                    last = tr(bank[6][:, t * P:(t + 1) * P], v_act[:, t * P:(t + 1) * P], ident)
                last.then_inc(v_turned, 1)
                project(0, i, b, 3, bank[3])
        with pe.Fori(0, H // 2) as i:
            for b in range(2):
                h = i * 2 + b
                pe.wait_ge(sq_done, h + 1)
                pe.wait_ge(norm_act, h * 2 + 2)
                mm(bank[b][:], ones[:], sq[:, b], start=True, stop=True).then_inc(sumsq_done, 1)
            for b in range(2):
                h = i * 2 + b
                pe.wait_ge(norm_set, h + 3)
                pe.wait_ge(pair_set, h * 6 + 6)
                pe.wait_ge(kd_set, h + 1)
                for t in range(TT):
                    both = kn[:, b].rearrange("p (a t c) -> p a t c", a=2, t=TT)[:, :, t, :]
                    mm(bank[2 + b][:, t * 2 * P:(t + 1) * 2 * P], kn[:, b, t * P:(t + 1) * P], both,
                       start=True, stop=True)
                tr(bank[4 + b][:, 0:P], kn[:, b, 0:P], ident).then_inc(pair_done, 1)

        def group(t, g, q):
            return t[:, g // 2, 4 * (g % 2) + q]

        for g in range(4):
            pe.wait_ge(masked, g + 1)
            for q in range(4):
                last = tr(bank[g][:, q * P:(q + 1) * P], group(LM, g, q), ident)
            last.then_inc(lm_turned, 1)
        with pe.Fori(0, LEVELS - 1) as j:
            for g in range(4):
                pe.wait_ge(masked, j * 4 + (5 + g))
                pe.wait_ge(inv_vec, j * 4 + (5 + g))
                pe.wait_ge(inv_act, j * 8 + (5 + g))
                for q in range(4):
                    last = mm(bank[g][:, q * P:(q + 1) * P], group(LM, g, q), group(U, g, q), start=True, stop=True)
                last.then_inc(inv_mm, 1)
            for g in range(4):
                pe.wait_ge(inv_act, j * 8 + (9 + g))
                for q in range(4):
                    last = mm(bank[4 + g][:, q * P:(q + 1) * P], group(TI, g, q), group(W, g, q),
                              start=True, stop=True)
                last.then_inc(inv_mm, 1)
            for g in range(4):
                pe.wait_ge(inv_vec, j * 4 + (9 + g))
                for q in range(4):
                    last = tr(bank[g][:, q * P:(q + 1) * P], group(U, g, q), ident)
                last.then_inc(inv_mm, 1)

        def heads(f, dst, n):
            for q in range(4):
                last = f(4 * n + q, dst[:, q * P:(q + 1) * P])
            last.then_inc(scan_mm, 1)

        pe.wait_ge(inv_act, 8 * LEVELS)
        pe.wait_ge(vb_done, 2 + 2 * H)
        for n in range(2):
            heads(lambda h, o: mm(o, U[:, 0, h], vb[:, 0, h], start=True, stop=True), bank[n], n)
        pe.wait_ge(kd_set, 2 + H)
        for n in range(2):
            pe.wait_ge(scan_act, n + 1)
            heads(lambda h, o: mm(o, kd0[:, h], V[:, 0, h], start=True, stop=True), bank[2 + n], n)
        for n in range(2):
            heads(lambda h, o: mm(o, V[:, 0, h], AT[:, 0, h], start=True, stop=True), bank[4 + n], n)
        for n in range(2):
            pe.wait_ge(scan_act, n + 3)
            heads(lambda h, o: mm(o, kT1[:, h], S1[:, h], start=True, stop=True), bank[6 + n], n)
        for n in range(2):
            pe.wait_ge(scan_vec, 2 + 4 * (n + 1))
            heads(lambda h, o: mm(o, U[:, 1, h], R[:, h], start=True, stop=True), bank[n], n)

        def second_out(h, o):
            mm(o, S1[:, h], qd1[:, h], start=True, stop=False)
            return mm(o, V[:, 1, h], AT[:, 1, h], start=False, stop=True)

        for n in range(2):
            pe.wait_ge(scan_act, n + 5)
            heads(second_out, bank[2 + n], n)
        for n in range(4):
            pe.wait_ge(rms_act, n + 1)
            pe.wait_ge(scan_vec, 10 if n >= 2 else 2)
            mm(bank[4 + n][:], ones[:], osq[:, 2 * n:2 * n + 2].rearrange("p a t -> p (a t)"),
               start=True, stop=True).then_inc(rms_mm, 1)

        def prob_turn(h):
            pe.wait_ge(att_vec, h * 9 + 7)
            for n in range(3):
                last = tr(bank[5][:, n * P:(n + 1) * P], prob[:, n], ident)
            last.then_inc(p_turned, 1)

        def prob_value(h):
            pe.wait_ge(probT_set, h + 1)
            pe.wait_ge(v_set, h + 1)
            if not (isinstance(h, int) and h == 0):
                pe.wait_ge(yalo_set, h)
            mm(bank[6][:, 0:P], v_nat[:, 0], probT[:, 0], start=True, stop=True)
            mm(bank[6][:, P:T], v_nat[:, 0], probT[:, 1], start=True, stop=False)
            mm(bank[6][:, P:T], v_nat[:, 1], probT[:, 2], start=False, stop=True).then_inc(pv_done, 1)

        def attend(i, b, first=False):
            h = i * 2 + b
            if not first:
                pe.wait_ge(qk_set, h * 2)
            project(1, i, b, 0, bank[0])
            if not first:
                prob_turn(h - 1)
            project(1, i, b, 1, bank[1])
            if not first:
                pe.wait_ge(vT_set, h)
            project(1, i, b, 2, bank[2])
            if not first:
                prob_value(h - 1)
            pe.wait_ge(qk_set, h * 2 + 2)
            if not first:
                pe.wait_ge(att_vec, h * 9 - 8)
            mm(bank[4][:, 0:P], qkT[:, 0, 0:P], qkT[:, 1, 0:P], start=True, stop=True)
            mm(bank[4][:, P:3 * P], qkT[:, 0, P:T], qkT[:, 1, :], start=True, stop=True).then_inc(score_done, 1)
            if not first:
                pe.wait_ge(ga_set, h)
                
            project(1, i, b, 3, bank[3])
            pe.wait_ge(vT_set, h + 1)
            for t in range(TT):
                last = tr(bank[7][:, t * P:(t + 1) * P], vT[:, t * P:(t + 1) * P], ident)
            last.then_inc(vT_turned, 1)

        pe.wait_ge(scan_vec, 12)
        pe.wait_ge(rms_act, 8)
        attend(0, 0, first=True)
        attend(0, 1)
        with pe.Fori(1, H // 2) as i:
            for b in range(2):
                attend(i, b)
        prob_turn(H - 1)
        prob_value(H - 1)

        def project_out(b, last_one=False):
            wide = [w[:, 1].rearrange("p k c -> p (k c)") for w in (whi, wlo)]
            for t in range(TT):
                for s in range(2):
                    last = three(bank[4 + 2 * t + s][:], [m[:, b, t * P:(t + 1) * P] for m in (mhi, mlo)],
                                 [w[:, s * 512:(s + 1) * 512] for w in wide], False, False)
                if last_one:
                    last.then_inc(mixed, 1)
            if not last_one:
                last.then_inc(proj_done, 1)

        def merge(i, b, first=False):
            h = i * 2 + b
            if not first:
                pe.wait_ge(gb_set, h)
            project(2, i, b, 0, bank[0])
            split_in(2, i, b, 1)
            if first:
                for n in range(4):
                    last = mm(bank[4 + n][:], zeros[:, 0:P], zeros[:], start=True, stop=False, skip_group_check=True)
                last.then_inc(proj_done, 1)
            else:
                pe.wait_ge(mlo_set, h)
                project_out(1 - b)
                pe.wait_ge(mer_vec, h * 5)
            project(2, i, b, 2, bank[1], rhs=(szhi, szlo))
            project(2, i, b, 3, bank[2], rhs=(yahi, yalo))

        pe.wait_ge(vT_set, H)
        pe.wait_ge(yalo_set, H)
        pe.wait_ge(v_set, H)
        pe.wait_ge(probT_set, H)
        pe.wait_ge(szlo_set, 4)
        pe.wait_ge(const_set, 7)
        merge(0, 0, first=True)
        merge(0, 1)
        with pe.Fori(1, H // 2) as i:
            for b in range(2):
                merge(i, b)
        pe.wait_ge(wlo_set[1], 2 * 3 * H + 1)
        pe.wait_ge(mlo_set, H)
        project_out(1, last_one=True)

        for t in range(TT):
            pe.wait_ge(ln_vec, LN_TILE * (t + 1))
            for m in range(2):
                for n in range(4):
                    k = 4 * m + n
                    last = tr(bank[2 * t + m][:, n * P:(n + 1) * P], x_nat[:, t, k * P:(k + 1) * P], ident)
                last.then_inc(x1_turned, 1)
            pe.wait_ge(rout_in, 32)
            pe.wait_ge(x1T_act, 2 + t)
            if t == 1:
                pe.wait_ge(x1T_vec, 1)
            for k in range(KC):
                last = mm(bank[4 + 2 * t][0:NE, 0:P], w_rout[:, k], x1T[:, k, t * P:(t + 1) * P],
                          start=(k == 0), stop=(k == KC - 1))
            last.then_inc(log_done, 1)
        for t in range(TT):
            pe.wait_ge(logT_set, t + 1)
            tr(bank[5 + 2 * t][:, 0:NE], logT[:, t * P:(t + 1) * P], ident[0:NE, 0:NE]).then_inc(log_turned, 1)

        def shared(n, dst, f, ks):
            for k in ks:
                last = mm(dst[:, f * T:(f + 1) * T], w_gu_s[:, n, k, f * P:(f + 1) * P], x1T[:, k],
                          start=(k == 0), stop=(k == KC - 1))
            return last

        pe.wait_ge(shared_in[0], 16)
        shared(0, bank[3], 0, range(KC))
        shared(0, bank[3], 1, range(KC)).then_inc(sh_done, 1)
        pe.wait_ge(sco_set, TT)
        for n in range(4):
            mm(bank[4 + n][:], zeros[:, 0:P], zeros[:], start=True, stop=False, skip_group_check=True)
        pe.wait_ge(rout_step, ROUT_SEL)
        mm(bank[2][:, 0:NE], c("before"), selm[:, 0], start=True, stop=True)
        mm(bank[2][:, NE:2 * NE], c("before"), selm[:, 1], start=True, stop=False)
        mm(bank[2][:, NE:2 * NE], ones[:], selm[:, 0], start=False, stop=True)
        mm(bank[2][:, 2 * NE:3 * NE], ones[:], selm[:, 0], start=True, stop=False)
        mm(bank[2][:, 2 * NE:3 * NE], ones[:], selm[:, 1], start=False, stop=True).then_inc(pos_done, 1)
        pe.wait_ge(shared_in[1], 16)
        shared(1, bank[0], 0, range(4))

        def shared_down(t, n):
            for f in range(2):
                mm(bank[4 + 2 * t + n][:], hsT[:, f, t * P:(t + 1) * P], w_d_s[:, f, n * 512:(n + 1) * 512],
                   start=False, stop=False, skip_group_check=True)

        def gather(step):
            for c2 in range(2):
                k = 2 * step + c2
                for n in range(4):
                    last = mm(bank[3][:, c2 * 256:(c2 + 1) * 256], x1r[:, n // 2, n % 2, k], pick[:, n // 2],
                              start=(n == 0), stop=(n == 3))
            last.then_inc(gath_done, 1)

        def scatter(b, part):
            for n in part:
                t, s, half = n // 4, n // 2 % 2, n % 2
                last = mm(bank[4 + 2 * t + s][:], drop[:, b, t * P:(t + 1) * P], yr[:, half, s * 512:(s + 1) * 512],
                          start=False, stop=False, skip_group_check=True)
            return last

        def pair_step(q, i, m, shared_too=False):
            b, n = m % 2, i * 2 + m // 2
            j = q * PAIRS + (i * 4 + m)
            slot = 6 * b
            for a in range(2):
                for w in range(2):
                    pe.wait_ge(exp_in[slot + 3 * a + w], q * 256 + i * 32 + (m // 2) * 16 + 16)
            pe.wait_ge(xg_set, q * 68 + n * 4 + 4)
            pe.wait_ge(hid_set, j + 1)
            tokens = xg[m // 2][:, b]
            for k in range(KC):
                for a in range(2):
                    last = mm(bank[0][64 * a:64 * a + 64, :], tokens[:, k, 64 * a:64 * a + 64],
                              ring[:, slot + 3 * a:slot + 3 * a + 2, k * FE:(k + 1) * FE],
                              start=(k == 0), stop=(k == KC - 1))
                if k == 1:
                    pe.wait_ge(pick_set, q * 72 + n * 4 + 6)
                    pe.wait_ge(hidT_set, j + 1)
                    gather(2 * b)
                if k == 4:
                    pe.wait_ge(xg_set, q * 68 + n * 4 + (5 + 2 * b))
                    gather(2 * b + 1)
                if k == 6:
                    pe.wait_ge(xg_set, q * 68 + n * 4 + (6 + 2 * b))
                    for t in range(TT):
                        turned = tr(bank[3][:, t * P:(t + 1) * P],
                                    wpick[:, m // 2, t, b * P:(b + 1) * P], ident)
                    turned.then_inc(wp_turned, 1)
            last.then_inc(gu_done, 1)
            pe.wait_ge(ylo_set, j * 2 + 2)
            pe.wait_ge(drop_set, j * 2 + 2)
            scatter(1 - b, range(6))
            if shared_too:
                shared_down(m // 2, m % 2)
            pe.wait_ge(hid_set, j + 2)
            pe.wait_ge(drop_set, j * 2 + 4)
            for f in range(2):
                last = tr(bank[3][:, f * P:(f + 1) * P], hid[:, f], ident)
            last.then_inc(hid_turned, 1)
            scatter(1 - b, range(6, 8)).then_inc(scat_done, 1)
            pe.wait_ge(hidT_set, j + 2)
            for a in range(2):
                pe.wait_ge(exp_in[slot + 3 * a + 2], q * 256 + i * 32 + (m // 2) * 16 + 16)
            for s in range(2):
                for f in range(2):
                    for a in range(2):
                        last = mm(bank[1 + s][64 * a:64 * a + 64, :], hidT[:, f, 64 * a:64 * a + 64],
                                  ring[:, slot + 3 * a + 2, f * D + s * 512:f * D + (s + 1) * 512],
                                  start=(f == 0), stop=(f == 1))
            last.then_inc(down_done, 1)

        def expert_pass(q, shared_too=False):
            for step in range(4):
                pe.wait_ge(pick_set, q * 72 + 2)
                if step == 0:
                    pe.wait_ge(hidT_set, q * PAIRS + 1)
                else:
                    pe.wait_ge(xg_set, q * 68 + step)
                gather(step)
                if shared_too and step < 3:
                    f, half = (step + 1) // 2, (step + 1) % 2
                    last = shared(1, bank[0], f, range(4 * half, 4 * half + 4))
                    if step == 2:
                        last.then_inc(sh_done, 1)
            if shared_too:
                pe.wait_ge(hsT_set, 1)
                pe.wait_ge(shared_in[2], 16)
                for m in range(4):
                    pair_step(q, 0, m, shared_too=True)
            with pe.Fori(1 if shared_too else 0, NE // 8) as i:
                for m in range(4):
                    pair_step(q, i, m)

        def last_pair(passes):
            pe.wait_ge(ylo_set, passes * PAIRS * 2 + 2)
            pe.wait_ge(drop_set, passes * PAIRS * 2 + 2)
            for t in range(TT):
                scatter(1, range(4 * t, 4 * t + 4)).then_inc(acc_done, 1)

        pe.wait_ge(clear_set, 2)
        pe.wait_ge(x1hi_set, 2)
        pe.wait_ge(x1lo_set, 2)
        pe.wait_ge(gsh_set, 1)
        expert_pass(0, shared_too=True)
        with pe.If(pe.value_load(most_i[0:1, 0:1], min_val=0, max_val=T) > SLOTS):
            with pe.Fori(1, PASSES) as q:
                expert_pass(q)
            last_pair(PASSES)
        with pe.Else():
            last_pair(1)

    @block.scalar
    def _(act):
        A = nc.scalar.activation
        act.sem_inc(act_done, 4)
        act.sem_inc(vb_done, 2)
        act.sem_inc(norm_act, 4)
        act.sem_inc(kd_set, 2)
        act.sem_inc(inv_act, 8)
        act.sem_inc(hidT_set, 1)
        nc.scalar.preload_act_table_set("natural_log_exp_and_others")
        for b in range(4):
            act.wait_ge(xT_vec, b + 1)
            A(xhi[:, 2 * b:2 * b + 2], xT[:, 2 * b:2 * b + 2], ACT.Copy).then_inc(xhi_set, 1)

        def split_first(b, value, k):
            act.wait_ge(mix_in[b][k], value)
            A(whi[:, k].rearrange("p k c -> p (k c)"), mixw[:, b, k].rearrange("p k c -> p (k c)"),
              ACT.Copy).then_inc(whi_set, 1)

        def split_next(phase, i, b, k):
            act.wait_ge(proj_done, i * 8 + (4 * (H * phase + b) + k + 1))
            split_first(1 - b, i * 16 + 16 * (H // 2 * phase + 1 + b), k)

        act.wait_ge(vec_in, 48)
        act.wait_ge(gate_vec, 3)
        s = Steps(act, gate_act)
        s.then(A(g_e[:, :, 0:H], g_abs[:], ACT.Exp, scale=-1.0))
        act.wait_ge(const_set, 6)
        s.did(A(g_e[:, :, 0:H], g_e[:, :, 0:H], ACT.Ln, bias=one[:]))
        s.did(A(alog[:], alog[:], ACT.Exp))
        s.did(A(g_e[:, :, H:16], ab[:, :, H:16], ACT.Exp, scale=-1.0))
        for k in range(4):
            split_first(0, 16, k)
        act.wait_ge(gate_vec, GATE_CUM)
        s.did(A(e_last[:], e_last[:], ACT.Exp))
        s.did(A(nbeg[:], gcl[:, 0], ACT.Exp))
        for n in range(TT * H):
            act.wait_ge(wide_done, n // 4 + 1)
            A(edist[:, n], bank[n // 4][:, (n % 4) * P:(n % 4 + 1) * P], ACT.Abs,
              bias=ngc[:, n:n + 1]).then_inc(dist_done, 1)
        for n in range(2):
            A(qd1[:, 4 * n:4 * n + 4].rearrange("p h c -> p (h c)"), bank[2 + n][:], ACT.Exp).then_inc(dist_done, 1)
        act.wait_ge(dist_done, 18)
        A(edist[:], edist[:], ACT.Exp, scale=-1.0).then_inc(dist_done, 1)

        nc.scalar.preload_act_table_set("silu_and_others")
        act.wait_ge(gate_vec, GATE_ALL)
        with act.Fori(0, H // 2) as i:
            for b in range(2):
                h = i * 2 + b
                split_next(0, i, b, 0)
                act.wait_ge(conv_step, h * 12 + 16)
                act.wait_ge(v_turned, h + 1)
                A(v_act[:], acc[:, 0], ACT.Silu).then_inc(act_done, 1)
                for n in range(2):
                    split_next(0, i, b, n + 1)
                    act.wait_ge(conv_step, h * 12 + (12 + 4 * (n + 2)))
                    A(kq[:, bass.ds(h, 1), n * T:(n + 1) * T].rearrange("p a t -> p (a t)"), acc[:, n + 1],
                      ACT.Silu).then_inc(act_done, 1)
                act.wait_ge(v_turned, h + 2)
                for t in range(TT):
                    A(vb[:, t, bass.ds(h, 1)].rearrange("p a c -> p (a c)"), bank[6][:, t * P:(t + 1) * P], ACT.Copy,
                      scale=beta[:, t, bass.ds(h, 1)]).then_inc(vb_done, 1)
                split_next(0, i, b, 3)
                A(szT[:, bass.ds(h, 1)].rearrange("p a t -> p (a t)"), bank[3][:, 0:T], ACT.Silu).then_inc(act_done, 1)

        nc.scalar.preload_act_table_set("natural_log_exp_and_others")
        act.wait_ge(act_done, 4 + 4 * H)
        with act.Fori(0, H // 2) as i:
            for b in range(2):
                A(sq[:, b], kq[:, bass.ds(i * 2 + b, 1)].rearrange("p a t -> p (a t)"), ACT.Square).then_inc(sq_done, 1)
            for b in range(2):
                h = i * 2 + b
                act.wait_ge(sumsq_done, h + 1)
                act.wait_ge(norm_set, h + 1)
                A(rr[:, b], bank[b][:], ACT.Ln, bias=eps_l2[:]).then_inc(norm_act, 1)
                act.wait_ge(norm_act, h * 2 + 5)
                A(rr[:, b], rr[:, b], ACT.Exp, scale=-0.5).then_inc(norm_act, 1)
            for b in range(2):
                h = i * 2 + b
                act.wait_ge(pair_done, h + 3)
                A(kd0[:, bass.ds(h, 1)].rearrange("p a c -> p (a c)"), bank[4 + b][:, 0:P], ACT.Copy,
                  scale=e_last[:, bass.ds(h, 1)]).then_inc(kd_set, 1)

        def rows(t, g):
            return t[:, g // 2, 4 * (g % 2):4 * (g % 2) + 4].rearrange("p h c -> p (h c)")

        with act.Fori(0, LEVELS - 1) as j:
            for g in range(4):
                act.wait_ge(inv_mm, j * 12 + (13 + g))
                A(rows(W, g), bank[g][:], ACT.Copy).then_inc(inv_act, 1)
            for g in range(4):
                act.wait_ge(inv_mm, j * 12 + (21 + g))
                A(rows(TI, g), bank[g][:], ACT.Copy).then_inc(inv_act, 1)

        def four(t, n):
            return t[:, 4 * n:4 * n + 4].rearrange("p h c -> p (h c)")

        for n in range(2):
            act.wait_ge(scan_mm, n + 1)
            A(four(V[:, 0], n), bank[n][:], ACT.Copy).then_inc(scan_act, 1)
        for n in range(2):
            act.wait_ge(scan_mm, n + 3)
            A(four(S1, n), bank[2 + n][:], ACT.Copy).then_inc(scan_act, 1)
        for n in range(2):
            act.wait_ge(scan_mm, n + 9)
            A(four(V[:, 1], n), bank[n][:], ACT.Copy).then_inc(scan_act, 1)
        act.wait_ge(scan_mm, SCAN_MM)
        act.wait_ge(scan_vec, 12)
        def pair(t, n):
            return t[:, 2 * n:2 * n + 2].rearrange("p h t -> p (h t)")

        for n in range(4):
            A(pair(osq, n), pair(oT, n), ACT.Square).then_inc(rms_act, 1)
        for n in range(4):
            act.wait_ge(rms_mm, n + 1)
            A(pair(osq, n), bank[4 + n][:], ACT.Ln, scale=1.0 / DH, bias=eps_rms[:]).then_inc(rms_act, 1)
        act.wait_ge(rms_act, 8)
        for n in range(4):
            A(pair(osq, n), pair(osq, n), ACT.Exp, scale=-0.5).then_inc(rms_act, 1)

        for n in range(4):
            act.wait_ge(rms_vec, n + 5)
            A(pair(szhi, n), pair(szT, n), ACT.Copy).then_inc(szhi_set, 1)

        def prob_out(h):
            if not (isinstance(h, int) and h == 0):
                act.wait_ge(pv_done, h)
            act.wait_ge(p_turned, h + 1)
            A(probT[:].rearrange("p a c -> p (a c)"), bank[5][:, 0:3 * P], ACT.Copy).then_inc(probT_set, 1)

        def value_out(h):
            act.wait_ge(pv_done, h + 1)
            A(yahi[:, bass.ds(h, 1)].rearrange("p a t -> p (a t)"), bank[6][:, 0:T], ACT.Copy).then_inc(yahi_set, 1)

        def attend(i, b, first=False):
            h = i * 2 + b
            for n in range(2):
                split_next(1, i, b, n)
                if n == 0 and not first:
                    act.wait_ge(score_done, h)
                A(qkT[:, n], bank[n][:, 0:T], ACT.Copy).then_inc(qk_set, 1)
            if not first:
                prob_out(h - 1)
            split_next(1, i, b, 2)
            if not first:
                act.wait_ge(vT_turned, h)
            A(vT[:], bank[2][:, 0:T], ACT.Copy).then_inc(vT_set, 1)
            if not first:
                value_out(h - 1)
            act.wait_ge(att_vec, h * 9 + 4)
            A(prob[:, 0], score[:, 0], ACT.Exp, bias=smx[:, 2:3], accum_out=smx[:, 4:5]).then_inc(exp_set, 1)
            A(prob[:, 1:3].rearrange("p a c -> p (a c)"), score[:, 1:3].rearrange("p a c -> p (a c)"), ACT.Exp,
              bias=smx[:, 3:4], accum_out=smx[:, 5:6]).then_inc(exp_set, 1)
            split_next(1, i, b, 3)
            if not first:
                act.wait_ge(att_vec, h * 9)
            A(gtmp[:, 0], bank[3][:, 0:T], ACT.Exp, scale=-1.0).then_inc(ga_set, 1)
            act.wait_ge(vT_turned, h + 1)
            A(v_nat[:].rearrange("p t c -> p (t c)"), bank[7][:, 0:T], ACT.Copy).then_inc(v_set, 1)

        nc.scalar.preload_act_table_set("exp_and_others")
        attend(0, 0, first=True)
        attend(0, 1)
        with act.Fori(1, H // 2) as i:
            for b in range(2):
                attend(i, b)
        prob_out(H - 1)
        value_out(H - 1)

        def merge(i, b, tiles=range(4)):
            h = i * 2 + b
            act.wait_ge(proj_done, i * 8 + (4 * (2 * H + b) + 1))
            if isinstance(h, int) and h == 0:
                act.wait_ge(att_vec, 9 * H)
            else:
                act.wait_ge(mer_vec, h * 5 - 2)
            A(gtmp[:, 0], bank[0][:, 0:T], ACT.Exp, scale=-1.0).then_inc(gb_set, 1)
            for k in tiles:
                split_next(2, i, b, k)
            act.wait_ge(mer_vec, h * 5 + 5)
            A(mhi[:, b], merged[:], ACT.Copy).then_inc(mhi_set, 1)

        for b in range(2):
            merge(0, b)
        with act.Fori(1, H // 2 - 1) as i:
            for b in range(2):
                merge(i, b)
        merge(H // 2 - 1, 0)
        merge(H // 2 - 1, 1, tiles=(1,))

        def deviation(t, vec, done):
            act.wait_ge(vec, LN_TILE * t + LN_STATS)
            A(moment[:, t, 1:2], moment[:, t, 1:2], ACT.Ln, bias=eps_ln[:]).then_inc(done, 1)
            act.wait_ge(done, 2 * t + 1)
            A(moment[:, t, 1:2], moment[:, t, 1:2], ACT.Exp, scale=-0.5).then_inc(done, 1)

        def turned_out(t, m):
            act.wait_ge(x1_turned, 2 * t + m + 1)
            A(x1T[:, 4 * m:4 * m + 4, t * P:(t + 1) * P], bank[2 * t + m][:].rearrange("p (k c) -> p k c", k=4),
              ACT.Copy).then_inc(x1T_act, 1)

        nc.scalar.preload_act_table_set("natural_log_exp_and_others")
        deviation(0, ln_vec, ln_act)
        turned_out(0, 0)
        turned_out(0, 1)
        deviation(1, ln_vec, ln_act)
        nc.scalar.preload_act_table_set("sigmoid_and_others")
        turned_out(1, 1)
        for t in range(TT):
            act.wait_ge(log_done, t + 1)
            A(logT[:, t * P:(t + 1) * P], bank[4 + 2 * t][0:NE, 0:P], ACT.Copy).then_inc(logT_set, 1)
        for t in range(TT):
            act.wait_ge(log_turned, t + 1)
            A(sco[:, t], bank[5 + 2 * t][:, 0:NE], ACT.Sigmoid).then_inc(sco_set, 1)
        for t in range(TT):
            A(x1r[:, t, 0].rearrange("p k q -> p q k"), x_nat[:, t].rearrange("p (q k) -> p q k", k=KC),
              ACT.Copy).then_inc(x1hi_set, 1)
        nc.scalar.preload_act_table_set("silu_and_others")
        act.wait_ge(sh_done, 1)
        A(gsh[:], bank[3][:], ACT.Silu).then_inc(gsh_set, 1)

        def evacuate(q, n, step, buffer):
            act.wait_ge(gath_done, q * 68 + n * 4 + (step + 1))
            A(xg[buffer][:, :, 2 * step:2 * step + 2].rearrange("p a k s -> p k a s"),
              bank[3][:].rearrange("p (k a s) -> p k a s", k=2, a=2), ACT.Copy).then_inc(xg_set, 1)

        def expert_pass(q):
            act.wait_ge(gu_done, q * PAIRS + 1)
            for step in range(4):
                evacuate(q, 0, step, 0)
            with act.Fori(0, NE // 8) as i:
                for m in range(4):
                    b, n = m % 2, i * 2 + m // 2
                    j = q * PAIRS + (i * 4 + m)
                    act.wait_ge(gu_done, j + (1 - b))
                    evacuate(q, n + 1, 2 * b, 1 - m // 2)
                    evacuate(q, n + 1, 2 * b + 1, 1 - m // 2)
                    act.wait_ge(gu_done, j + 2)
                    act.wait_ge(hid_set, j + 1)
                    A(gact[:], bank[0][:, 0:FE], ACT.Silu).then_inc(act_set, 1)
                    act.wait_ge(hid_turned, j + 1)
                    A(hidT[:].rearrange("p f s -> p (f s)"), bank[3][:, 0:2 * P], ACT.Copy).then_inc(hidT_set, 1)
                    act.wait_ge(down_done, j + 1)
                    act.wait_ge(drop_set, j * 2 + 4)
                    for s in range(2):
                        A(yr[:, 0, s * 512:(s + 1) * 512], bank[1 + s][:], ACT.Copy,
                          scale=wslot[:, b:b + 1]).then_inc(yhi_set, 1)

        expert_pass(0)
        with act.If(act.value_load(most_i[0:1, 0:1], min_val=0, max_val=T) > SLOTS):
            with act.Fori(1, PASSES) as q:
                expert_pass(q)

        nc.scalar.preload_act_table_set("natural_log_exp_and_others")
        for t in range(TT):
            deviation(t, ln2_vec, ln2_act)

    @block.gpsimd
    def _(pool):
        def split_second(b, value, k):
            pool.wait_ge(whi_set, value)
            nc.gpsimd.tensor_tensor(wlo[:, k], mixw[:, b, k], whi[:, k].bitcast(F32), ALU.subtract).then_inc(
                wlo_set[1], 1)

        with pool.Fori(0, 3 * H // 2) as i:
            for b in range(2):
                for k in (1, 3):
                    split_second(b, i * 8 + (4 * b + k + 1), k)
        split_second(0, 4 * 3 * H + 1, 1)
        pool.wait_ge(ln_vec, LN_TILE)
        nc.gpsimd.memset(drop[:].bitcast(F32), 0.0).then_inc(clear_set, 1)
        nc.gpsimd.memset(yr[:].bitcast(F32), 0.0).then_inc(clear_set, 1)
        for t in range(TT):
            pool.wait_ge(x1hi_set, t + 1)
            nc.gpsimd.tensor_tensor(x1r[:, t, 1].rearrange("p k q -> p q k"),
                                    x_nat[:, t].rearrange("p (q k) -> p q k", k=KC),
                                    x1r[:, t, 0].bitcast(F32).rearrange("p k q -> p q k"),
                                    ALU.subtract).then_inc(x1lo_set, 1)

    @block.vector
    def _(dve):
        v = nc.vector
        dve.sem_inc(conv_step, 12)
        dve.sem_inc(norm_set, 2)
        dve.sem_inc(pair_set, 12)
        dve.sem_inc(hid_set, 1)
        dve.sem_inc(ylo_set, 2)
        dve.sem_inc(drop_set, 2)
        for t, value in ((ones[:], 1.0), (one[:], 1.0), (eps_l2[:], L2_EPS), (eps_rms[:], RMS_EPS),
                         (eps_ln[:], LN_EPS), (smx[:], 0.0)):
            v.memset(t, value).then_inc(const_set, 1)
        for b in range(4):
            dve.wait_ge(x_turned, b + 1)
            v.tensor_copy(xT[:, 2 * b:2 * b + 2].rearrange("p k t -> p (k t)"), bank[b][:]).then_inc(xT_vec, 1)
        dve.wait_ge(x_turned, 5)
        v.tensor_copy(conv_w[:], bank[4][:, 0:96]).then_inc(xT_vec, 1)
        dve.wait_ge(ab_done, 1)
        v.tensor_copy(abT[:], bank[5][0:16, 0:T]).then_inc(ab_set, 1)
        s = Steps(dve, gate_vec)
        dve.wait_ge(ab_done, 2)
        s.then(v.tensor_copy(ab[:].rearrange("p t n -> p (t n)"), bank[6][:, 0:32]))
        dve.wait_ge(vec_in, 48)
        per_head = [P, TT, H]
        s.then(v.tensor_tensor(g_u[:], ab[:, :, 0:H], dtb[:].unsqueeze(1).to_broadcast(per_head), ALU.add))
        s.then(v.scalar_tensor_tensor(g_abs[:], g_u[:], -1.0, g_u[:], ALU.mult, ALU.max))
        dve.wait_ge(gate_act, 4)
        s.then(v.scalar_tensor_tensor(g_u[:], g_u[:], 0.0, g_e[:, :, 0:H], ALU.max, ALU.add))
        s.then(v.scalar_tensor_tensor(decay_g[:], g_u[:], -1.0, alog[:].unsqueeze(1).to_broadcast(per_head),
                                      ALU.mult, ALU.mult))
        assert s.count == GATE_G
        s.did(v.tensor_copy(g_wide[:], decay_g[:].rearrange("p t h -> p (t h)").unsqueeze(2).to_broadcast(
            [P, TT * H, P])))
        assert s.count == GATE_WIDE
        for b in range(4):
            dve.wait_ge(xhi_set, b + 1)
            dve.wait_ge(xT_vec, b + 1)
            part = slice(2 * b, 2 * b + 2)
            v.tensor_tensor(xlo[:, part], xT[:, part], xhi[:, part].bitcast(F32), ALU.subtract).then_inc(xlo_set, 1)
        s.then(v.tensor_scalar(beta[:], g_e[:, :, H:16], 1.0, None, ALU.add))
        s.then(v.reciprocal(beta[:], beta[:]))
        dve.wait_ge(cum_done, 1)
        s.then(v.tensor_copy(gcl[:].rearrange("p a n -> p (a n)"), bank[7][:, 0:32]))
        s.did(v.tensor_scalar(ngc[:], gcl[:, 0], -1.0, None, ALU.mult))
        s.did(v.tensor_tensor(e_last[:], gcl[:, 1], gcl[:, 0], ALU.subtract))
        assert s.count == GATE_CUM
        dve.wait_ge(gate_act, 6)
        s.did(v.scalar_tensor_tensor(nbeg[:], nbeg[:], -1.0, beta[:].rearrange("p t h -> p (t h)"),
                                     ALU.mult, ALU.mult))
        def split_second(b, value, k):
            dve.wait_ge(whi_set, value)
            v.tensor_tensor(wlo[:, k], mixw[:, b, k], whi[:, k].bitcast(F32), ALU.subtract).then_inc(wlo_set[0], 1)

        def split_next(phase, i, b, k):
            split_second(1 - b, i * 8 + (4 * (H * phase + b + 1) + k + 1), k)

        for k in (0, 2):
            split_second(0, k + 1, k)
        dve.wait_ge(dist_done, 19)
        wide = [P, TT * H, P]
        s.did(v.scalar_tensor_tensor(AT[:].rearrange("p t h c -> p (t h) c"), edist[:], QK_SCALE,
                                     c("tri").unsqueeze(1).to_broadcast(wide), ALU.mult, ALU.mult))
        s.did(v.tensor_tensor(L[:].rearrange("p t h c -> p (t h) c"), edist[:],
                              c("strict").unsqueeze(1).to_broadcast(wide), ALU.mult))
        assert s.count == GATE_ALL

        dve.wait_ge(xT_vec, 5)
        s = Steps(dve, conv_step)
        s.count = 12
        with dve.Fori(0, H // 2) as i:
            s.enter(i, 24)
            for b in range(2):
                h = i * 2 + b
                for n, first in enumerate((16, 8, 0)):
                    def tap(j):
                        return conv_w[:, bass.ds(h + (j * 24 + first), 1)]
                    dve.wait_ge(proj_done, h * 4 + (n + 1))
                    dve.wait_ge(act_done, h * 4 + (n + 1))
                    s.then(v.tensor_scalar(acc[:, n], bank[n][:, 0:T], tap(3), None, ALU.mult))
                    for d in range(1, 4):
                        f = s.then if d < 3 else s.did
                        f(v.scalar_tensor_tensor(acc[:, n, d:T], bank[n][:, 0:T - d], tap(3 - d), acc[:, n, d:T],
                                                 ALU.mult, ALU.add))
                    if n != 1:
                        split_next(0, i, b, n)
            s.leave(H // 2)

        def row(t, h):
            return t[:, bass.ds(h, 1)].rearrange("p a c -> p (a c)")

        dve.wait_ge(v_turned, 1 + H)
        with dve.Fori(0, H // 2) as i:
            for b in range(2):
                h = i * 2 + b
                dve.wait_ge(norm_act, h * 2 + 6)
                dve.wait_ge(pair_done, h + 1)
                dve.wait_ge(pair_set, h * 6 + 6)
                v.tensor_tensor(kn[:, b], row(kq, h), rr[:, b], ALU.mult).then_inc(norm_set, 1)
            for b in range(2):
                h = i * 2 + b
                dve.wait_ge(norm_set, h + 3)
                dve.wait_ge(pair_done, h + 3)
                for t in range(TT):
                    both = bank[2 + b][:, t * 2 * P:(t + 1) * 2 * P]
                    v.scalar_tensor_tensor(row(L[:, t], h), both[:, 0:P], beta[:, t, bass.ds(h, 1)],
                                           row(L[:, t], h), ALU.mult, ALU.mult).then_inc(pair_set, 1)
                    v.tensor_tensor(row(AT[:, t], h), both[:, P:2 * P], row(AT[:, t], h),
                                    ALU.mult).then_inc(pair_set, 1)
                v.tensor_copy(row(kT1, h), kn[:, b, P:T]).then_inc(pair_set, 1)
                v.scalar_tensor_tensor(row(qd1, h), kn[:, b, T + P:2 * T], QK_SCALE, row(qd1, h),
                                       ALU.mult, ALU.mult).then_inc(pair_set, 1)

        def heads(t, g):
            return t[:, g // 2, 4 * (g % 2):4 * (g % 2) + 4]

        four = [P, 4, P]
        levels = c("levels", LEVELS)
        dve.wait_ge(pair_set, 12 + 6 * H)
        dve.wait_ge(act_done, 4 + 4 * H)
        for g in range(4):
            v.tensor_tensor(heads(LM, g), heads(L, g), levels[:, 0].unsqueeze(1).to_broadcast(four),
                            ALU.mult).then_inc(masked, 1)
        eye = ident.unsqueeze(1).to_broadcast(four)
        dve.wait_ge(masked, 4)
        for g in range(4):
            v.tensor_tensor(heads(TI, g), eye, heads(LM, g), ALU.subtract).then_inc(inv_vec, 1)
        for g in range(4):
            dve.wait_ge(lm_turned, g + 1)
            v.tensor_tensor(heads(U, g), eye, bank[g][:].rearrange("p (h c) -> p h c", h=4),
                            ALU.subtract).then_inc(inv_vec, 1)
        dve.wait_ge(inv_vec, 8)
        with dve.Fori(0, LEVELS - 1) as j:
            for g in range(4):
                dve.wait_ge(inv_mm, j * 12 + (1 + g))
                v.tensor_tensor(heads(LM, g), heads(L, g),
                                levels[:, bass.ds(j + 1, 1)].to_broadcast(four), ALU.mult).then_inc(masked, 1)
            for g in range(4):
                dve.wait_ge(inv_mm, j * 12 + (17 + g))
                v.tensor_tensor(heads(U, g), heads(U, g), bank[4 + g][:].rearrange("p (h c) -> p h c", h=4),
                                ALU.subtract).then_inc(inv_vec, 1)

        for n in range(2):
            dve.wait_ge(scan_mm, n + 5)
            v.tensor_copy(oT[:, 4 * n:4 * n + 4, 0:P], bank[4 + n][:].rearrange("p (h c) -> p h c", h=4)).then_inc(
                scan_vec, 1)
        for h in range(H):
            dve.wait_ge(scan_mm, h // 4 + 7)
            v.scalar_tensor_tensor(R[:, h], bank[6 + h // 4][:, (h % 4) * P:(h % 4 + 1) * P],
                                   nbeg[:, H + h:H + h + 1], vb[:, 1, h], ALU.mult, ALU.add).then_inc(scan_vec, 1)
        for n in range(2):
            dve.wait_ge(scan_mm, n + 11)
            v.tensor_copy(oT[:, 4 * n:4 * n + 4, P:T], bank[2 + n][:].rearrange("p (h c) -> p h c", h=4)).then_inc(
                scan_vec, 1)
        dve.wait_ge(scan_vec, 10)
        v.memset(zeros[:], 0.0).then_inc(const_set, 1)
        def pair(t, n):
            return t[:, 2 * n:2 * n + 2].rearrange("p h t -> p (h t)")

        for n in range(4):
            dve.wait_ge(rms_act, 9 + n)
            v.tensor_tensor(pair(oT, n), pair(oT, n), pair(osq, n), ALU.mult).then_inc(rms_vec, 1)
        for n in range(4):
            dve.wait_ge(rms_vec, n + 1)
            v.scalar_tensor_tensor(pair(szT, n), pair(oT, n), normw[:], pair(szT, n), ALU.mult,
                                   ALU.mult).then_inc(rms_vec, 1)

        for n in range(4):
            dve.wait_ge(szhi_set, n + 1)
            v.tensor_tensor(pair(szlo, n), pair(szT, n), pair(szhi, n).bitcast(F32), ALU.subtract).then_inc(szlo_set, 1)

        s = Steps(dve, att_vec)

        def value_low(h):
            dve.wait_ge(yahi_set, h + 1)
            v.tensor_tensor(row(yalo, h), bank[6][:, 0:T], row(yahi, h).bitcast(F32), ALU.subtract).then_inc(
                yalo_set, 1)

        def attend(i, b, first=False):
            h = i * 2 + b
            split_next(1, i, b, 0)
            if not first:
                value_low(h - 1)
            dve.wait_ge(score_done, h + 1)
            s.then(v.scalar_tensor_tensor(score[:].rearrange("p a c -> p (a c)"), bank[4][:, 0:3 * P], QK_SCALE,
                                          c("causal"), ALU.mult, ALU.add))
            s.did(v.tensor_reduce(smx[:, 0:1], score[:, 0], AX.X, ALU.max))
            s.then(v.tensor_reduce(smx[:, 1:2], score[:, 1:3].rearrange("p a c -> p (a c)"), AX.X, ALU.max))
            s.did(v.tensor_scalar(smx[:, 2:4], smx[:, 0:2], -1.0, None, ALU.mult))
            split_next(1, i, b, 2)
            dve.wait_ge(exp_set, h * 2 + 2)
            s.then(v.reciprocal(smx[:, 6:8], smx[:, 4:6]))
            s.did(v.tensor_scalar(prob[:, 0], prob[:, 0], smx[:, 6:7], None, ALU.mult))
            flat = prob[:, 1:3].rearrange("p a c -> p (a c)")
            s.did(v.tensor_scalar(flat, flat, smx[:, 7:8], None, ALU.mult))
            dve.wait_ge(ga_set, h + 1)
            s.then(v.tensor_scalar(gtmp[:, 0], gtmp[:, 0], 1.0, None, ALU.add))
            s.did(v.reciprocal(row(sga, h), gtmp[:, 0]))

        attend(0, 0, first=True)
        attend(0, 1)
        with dve.Fori(1, H // 2) as i:
            s.enter(i - 1, 18)
            for b in range(2):
                attend(i, b)
            s.leave(H // 2 - 1)
        value_low(H - 1)

        s.settle()
        s2 = Steps(dve, mer_vec)

        def merge(i, b, last=False):
            h = i * 2 + b
            dve.wait_ge(gb_set, h + 1)
            s2.then(v.tensor_scalar(gtmp[:, 0], gtmp[:, 0], 1.0, None, ALU.add))
            s2.then(v.reciprocal(gtmp[:, 0], gtmp[:, 0]))
            if not last:
                split_next(2, i, b, 0)
            dve.wait_ge(proj_done, i * 8 + (4 * (2 * H + b) + 3))
            s2.did(v.tensor_tensor(gtmp[:, 1], bank[1][:, 0:T], gtmp[:, 0], ALU.mult))
            if not last:
                split_next(2, i, b, 2)
            dve.wait_ge(proj_done, i * 8 + (4 * (2 * H + b) + 4))
            if not (isinstance(h, int) and h == 0):
                dve.wait_ge(mlo_set, h)
            s2.then(v.tensor_tensor(merged[:], bank[2][:, 0:T], row(sga, h), ALU.mult))
            s2.did(v.tensor_tensor(merged[:], merged[:], gtmp[:, 1], ALU.add))
            dve.wait_ge(mhi_set, h + 1)
            v.tensor_tensor(mlo[:, b], merged[:], mhi[:, b].bitcast(F32), ALU.subtract).then_inc(mlo_set, 1)

        for b in range(2):
            merge(0, b)
        with dve.Fori(1, H // 2 - 1) as i:
            s2.enter(i - 1, 10)
            for b in range(2):
                merge(i, b)
            s2.leave(H // 2 - 2)
        merge(H // 2 - 1, 0)
        merge(H // 2 - 1, 1, last=True)

        def layer_norm(ready, done, act_sem, gb):
            s = Steps(dve, done)
            for t in range(TT):
                dve.wait_ge(ready, t + 1)
                for n in range(2):
                    half = x_nat[:, t, n * 512:(n + 1) * 512]
                    s.did(v.scalar_tensor_tensor(half, half, ALPHA, bank[4 + 2 * t + n][:], ALU.mult, ALU.add))
                s.settle()
                for n in range(2):
                    s.did(v.bn_stats(stats[:, t, n], x_nat[:, t, n * 512:(n + 1) * 512]))
                s.settle()
                s.then(v.bn_aggr(moment[:, t], stats[:, t].rearrange("p n s -> p (n s)")))
                assert s.count == LN_TILE * t + LN_STATS
                s.then(v.scalar_tensor_tensor(x_nat[:, t], x_nat[:, t], moment[:, t, 0:1], gb[:, 0], ALU.subtract,
                                              ALU.mult))
                dve.wait_ge(act_sem, 2 * t + 2)
                s.did(v.scalar_tensor_tensor(x_nat[:, t], x_nat[:, t], moment[:, t, 1:2], gb[:, 1], ALU.mult,
                                             ALU.add))
                assert s.count == LN_TILE * (t + 1)

        dve.wait_ge(ln1_in, 32)
        layer_norm(mixed, ln_vec, ln_act, ln1v)

        dve.wait_ge(x1_turned, 3)
        v.tensor_copy(x1T[:, 0:4, P:T], bank[2][:].rearrange("p (k c) -> p k c", k=4)).then_inc(x1T_vec, 1)

        s = Steps(dve, rout_step)
        dve.wait_ge(sco_set, TT)
        dve.wait_ge(rout_in, 32)
        all_e, grouped = [P, TT, NE], [P, TT, GROUPS, NE // GROUPS]
        s.then(v.tensor_tensor(cho[:], sco[:], r_bias[:].unsqueeze(1).to_broadcast(all_e), ALU.add))
        for t in range(TT):
            for g in range(GROUPS):
                s.did(v.max(best[:, t, g], cho[:, t, g * 8:(g + 1) * 8]))
        s.settle()
        s.then(v.tensor_tensor(gsc[:], best[:, :, :, 0], best[:, :, :, 1], ALU.add))
        own, other = gsc[:].unsqueeze(3).to_broadcast([P, TT, 8, 8]), gsc[:].unsqueeze(2).to_broadcast([P, TT, 8, 8])
        s.did(v.tensor_tensor(cmp1[:], other, own, ALU.is_gt))
        s.then(v.tensor_tensor(cmp2[:], other, own, ALU.is_equal))
        tie = c("tie", GROUPS).unsqueeze(1).to_broadcast([P, TT, 8, 8])
        s.then(v.tensor_tensor(cmp2[:], cmp2[:], tie, ALU.mult))
        s.then(v.tensor_tensor(cmp1[:], cmp1[:], cmp2[:], ALU.add))
        s.then(v.tensor_reduce(gmk[:], cmp1[:], AX.X, ALU.add))
        s.then(v.tensor_scalar(gmk[:], gmk[:], TOP_G - 0.5, None, ALU.is_lt))
        s.did(v.tensor_scalar(goff[:], gmk[:], 1.0, -NEG, ALU.subtract, ALU.mult))
        by_group = cho[:].rearrange("p t (g e) -> p t g e", g=GROUPS)
        s.then(v.tensor_tensor(by_group, by_group, gmk[:].unsqueeze(3).to_broadcast(grouped), ALU.mult))
        s.then(v.tensor_tensor(by_group, by_group, goff[:].unsqueeze(3).to_broadcast(grouped), ALU.add))
        for t in range(TT):
            s.did(v.max(top[:, t], cho[:, t]))
        s.settle()
        for t in range(TT):
            s.did(v.match_replace(rep_[:, t], top[:, t], cho[:, t], 4 * NEG))
        s.settle()
        s.then(v.tensor_tensor(selm[:], rep_[:], cho[:], ALU.not_equal))
        assert s.count == ROUT_SEL, s.count
        s.then(v.tensor_tensor(sco[:], sco[:], selm[:], ALU.mult))
        s.then(v.tensor_reduce(wsum[:], sco[:], AX.X, ALU.add))
        s.then(v.reciprocal(wsum[:], wsum[:]))
        dve.wait_ge(pos_done, 1)
        s.then(v.tensor_reduce(most[:], bank[2][:, 2 * NE:3 * NE], AX.X, ALU.max))
        s.did(v.tensor_copy(most_i[:], most[:]))
        assert s.count == ROUT_MOST, s.count
        s.did(v.memset(pos[:], -1.0))
        s.then(v.memset(wgt[:], 0.0))
        for t in range(TT):
            s.did(v.tensor_scalar(wgt[:, t, 0:NE], sco[:, t], wsum[:, t:t + 1], ROUTED_SCALE, ALU.mult, ALU.mult))
        places = pos[:, :, 0:NE]
        s.then(v.scalar_tensor_tensor(places, bank[2][:, 0:2 * NE].rearrange("p (t e) -> p t e", t=TT), 1.0, selm[:],
                                      ALU.add, ALU.mult))
        s.then(v.tensor_scalar(places, places, 1.0, None, ALU.subtract))
        def places_of(first, buffer, before):
            spread = [P, BATCH, SLOTS]
            slots = c("slot").unsqueeze(1).to_broadcast(spread)
            for t in range(TT):
                v.tensor_tensor(pick[:, t].rearrange("p (e s) -> p e s", e=BATCH),
                                pos[:, t, bass.ds(first, BATCH)].unsqueeze(2).to_broadcast(spread), slots,
                                ALU.is_equal).then_inc(pick_set, 1)
            dve.wait_ge(pick_set, before + 2)
            for t in range(TT):
                v.tensor_tensor(wpick[:, buffer, t].rearrange("p (e s) -> p e s", e=BATCH),
                                pick[:, t].bitcast(F32).rearrange("p (e s) -> p e s", e=BATCH),
                                wgt[:, t, bass.ds(first, BATCH)].unsqueeze(2).to_broadcast(spread),
                                ALU.mult).then_inc(pick_set, 1)

        def expert_pass(q, shared_too=False):
            places_of(0, 0, q * 72)
            if shared_too:
                dve.wait_ge(gsh_set, 1)
                dve.wait_ge(sh_done, 2)
                v.tensor_tensor(hsT[:].rearrange("p f t -> p (f t)"), bank[0][:], gsh[:], ALU.mult).then_inc(hsT_set, 1)
            dve.wait_ge(gath_done, q * 68 + 4)
            dve.wait_ge(pick_set, q * 72 + 4)
            places_of(BATCH, 1, q * 72 + 4)
            with dve.Fori(0, NE // 8) as i:
                for m in range(4):
                    b, n = m % 2, i * 2 + m // 2
                    j = q * PAIRS + (i * 4 + m)
                    dve.wait_ge(wp_turned, j + 1)
                    dve.wait_ge(scat_done, j + 1)
                    v.tensor_scalar(drop[:, b], bank[3][:, 0:T], 0.0, None, ALU.is_gt).then_inc(drop_set, 1)
                    v.tensor_reduce(wslot[:, b:b + 1], bank[3][:, 0:T], AX.X, ALU.add).then_inc(drop_set, 1)
                    dve.wait_ge(act_set, j + 1)
                    v.tensor_tensor(hid[:].rearrange("p f s -> p s f"), gact[:].rearrange("p (s f) -> p s f", f=2),
                                    bank[0][:, FE:2 * FE].rearrange("p (s f) -> p s f", f=2),
                                    ALU.mult).then_inc(hid_set, 1)
                    if b == 1:
                        dve.wait_ge(gath_done, q * 68 + n * 4 + 8)
                        dve.wait_ge(pick_set, q * 72 + n * 4 + 8)
                        places_of(n * BATCH + 2 * BATCH, m // 2, q * 72 + n * 4 + 8)
                    for s in range(2):
                        dve.wait_ge(yhi_set, j * 2 + (s + 1))
                        part = slice(s * 512, (s + 1) * 512)
                        v.scalar_tensor_tensor(yr[:, 1, part], bank[1 + s][:], wslot[:, b:b + 1],
                                               yr[:, 0, part].bitcast(F32), ALU.mult,
                                               ALU.subtract).then_inc(ylo_set, 1)

        s.settle()
        expert_pass(0, shared_too=True)
        with dve.If(dve.value_load(most_i[0:1, 0:1], min_val=0, max_val=T) > SLOTS):
            with dve.Fori(1, PASSES) as q:
                dve.wait_ge(pick_set, q * 72)
                v.tensor_scalar(pos[:], pos[:], float(SLOTS), None, ALU.subtract).then_inc(rout_step, 1)
                dve.wait_ge(rout_step, q + s.count)
                expert_pass(q)

        dve.wait_ge(ln2_in, 32)
        layer_norm(acc_done, ln2_vec, ln2_act, ln2v)


_INS = ["x", "w_in", "dn_conv_w", "dn_a_log", "dn_dt_bias", "dn_norm_w", "w_branch_a", "w_branch_b", "w_out", "ln1_g",
        "ln1_b", "w_router", "router_bias", "w_gate_e", "w_up_e", "w_down_e", "w_gate_s", "w_up_s", "w_down_s",
        "ln2_g", "ln2_b"]


def kernel(**inputs):
    import concourse.bacc as bacc
    from concourse.bass_utils import run_bass_kernel_spmd

    nc = bacc.Bacc("TRN2", target_bir_lowering=False, num_devices=1)
    arrays = {f"in_{name}": np.ascontiguousarray(inputs[name]) for name in _INS}
    arrays["in_table"] = constants()
    args = [nc.dram_tensor(name, a.shape, mybir.dt.from_np(a.dtype), kind="ExternalInput").ap()
            for name, a in arrays.items()]
    out = nc.dram_tensor("out", inputs["x"].shape, F32, kind="ExternalOutput").ap()
    program(nc, *args, out)
    return run_bass_kernel_spmd(nc, [arrays], core_ids=[0]).results[0]["out"]
```
